# Optimizing a Trainium2 kernel written in Bass

```python
import math
import jax, jax.numpy as jnp
from jax import lax
import numpy as np

D_MODEL = 1024
BATCH = 1
SEQ = 512
DEPTH = 1
DEC_BATCH = 8
DEC_SEQ = 1
PAST_LEN = 1024
PAGE_SIZE = 128

N_GROUPS = 3
GROUP_WINDOWS = (128, 512, 2048)
GROUP_DILATIONS = (1, 4, 16)
HEADS_PER_GROUP = 8
HEAD_DIM = 64
ATTN_WIDTH = HEADS_PER_GROUP * HEAD_DIM
QKV_WIDTH = N_GROUPS * ATTN_WIDTH
CONV_CH = D_MODEL
CONV_WIDTH = 31
D_FF = 4 * D_MODEL
BLOCK = 128
IN_WIDTH = 3 * QKV_WIDTH + 2 * CONV_CH + 2 * D_MODEL
EPS = 1e-6
ATTN_SCALE = 1.0 / math.sqrt(HEAD_DIM)

kernel_name = "dilated_swa_conformer_conv_gated_hybrid_step"

def rmsnorm(x, g):
    xf = x.astype(jnp.float32)
    y = xf * lax.rsqrt(jnp.mean(xf * xf, axis=-1, keepdims=True) + EPS)
    return (y * g.astype(jnp.float32)).astype(x.dtype)

def layernorm(x, g, b):
    xf = x.astype(jnp.float32)
    mu = jnp.mean(xf, axis=-1, keepdims=True)
    var = jnp.mean(jnp.square(xf - mu), axis=-1, keepdims=True)
    y = (xf - mu) * lax.rsqrt(var + EPS)
    return (y * g.astype(jnp.float32) + b.astype(jnp.float32)).astype(x.dtype)

def mixer_inputs(x, norm1_g, w_in, q_norm_g, k_norm_g):
    B, T, _ = x.shape
    xn = rmsnorm(x, norm1_g)
    proj = xn @ w_in
    q, k, v, glu, gates = jnp.split(
        proj, [QKV_WIDTH, 2 * QKV_WIDTH, 3 * QKV_WIDTH, 3 * QKV_WIDTH + 2 * CONV_CH], axis=-1)
    hshape = (B, T, N_GROUPS, HEADS_PER_GROUP, HEAD_DIM)
    q = rmsnorm(q.reshape(hshape), q_norm_g[:, None, :])
    k = rmsnorm(k.reshape(hshape), k_norm_g[:, None, :])
    v = v.reshape(hshape)
    glu_a, glu_b = jnp.split(glu, 2, axis=-1)
    u = glu_a * jax.nn.sigmoid(glu_b)
    return q, k, v, u, gates

def dilated_attention_prompt(q, k, v, dilation, window):
    B, S, H, E = q.shape
    L = S // dilation
    n_keys = window // dilation
    nb = -(-L // BLOCK)
    Lp = nb * BLOCK
    N = B * dilation

    def to_blocks(t):
        t = t.reshape(B, L, dilation, H, E).transpose(0, 2, 1, 3, 4).reshape(N, L, H, E)
        t = jnp.pad(t, ((0, 0), (0, Lp - L), (0, 0), (0, 0)))
        return t.reshape(N, nb, BLOCK, H, E)

    def band(t):
        prev = jnp.pad(t[:, :-1], ((0, 0), (1, 0), (0, 0), (0, 0), (0, 0)))
        return jnp.concatenate([prev, t], axis=2)

    qb, kb, vb = to_blocks(q), to_blocks(k), to_blocks(v)
    kk, vv = band(kb), band(vb)
    s = jnp.einsum('nbqhe,nbkhe->nbhqk', qb.astype(jnp.float32), kk.astype(jnp.float32)) * ATTN_SCALE
    a = jnp.arange(BLOCK)[:, None]
    c = jnp.arange(2 * BLOCK)[None, :]
    dist = a + BLOCK - c
    blk = jnp.arange(nb)[:, None, None]
    valid = (dist >= 0) & (dist <= n_keys) & (blk * BLOCK - BLOCK + c >= 0)
    s = jnp.where(valid[None, :, None], s, -jnp.inf)
    lse = jax.nn.logsumexp(s, axis=-1)
    p = jnp.exp(s - lse[..., None])
    o = jnp.einsum('nbhqk,nbkhe->nbqhe', p, vv.astype(jnp.float32))
    o = o.reshape(N, Lp, H, E)[:, :L].reshape(B, dilation, L, H, E)
    o = o.transpose(0, 2, 1, 3, 4).reshape(B, S, H, E)
    lse = lse.transpose(0, 1, 3, 2).reshape(N, Lp, H)[:, :L].reshape(B, dilation, L, H)
    lse = lse.transpose(0, 2, 1, 3).reshape(B, S, H)
    return o, lse

def dilated_attention_sample(q, k_new, v_new, k_buf, v_buf, dilation, window):
    T = q.shape[1]
    Lb = k_buf.shape[1]
    kc = jnp.concatenate([k_buf, k_new], axis=1)
    vc = jnp.concatenate([v_buf, v_new], axis=1)
    m = jnp.arange(window // dilation + 1)
    idx = Lb + jnp.arange(T)[:, None] - m[None, :] * dilation
    valid = idx >= 0
    idx = jnp.clip(idx, 0)
    kg = kc[:, idx]
    vg = vc[:, idx]
    s = jnp.einsum('bthe,btmhe->bhtm', q.astype(jnp.float32), kg.astype(jnp.float32)) * ATTN_SCALE
    s = jnp.where(valid[None, None], s, -jnp.inf)
    lse = jax.nn.logsumexp(s, axis=-1)
    p = jnp.exp(s - lse[..., None])
    o = jnp.einsum('bhtm,btmhe->bthe', p, vg.astype(jnp.float32))
    keep = min(window, Lb + T)
    return o, lse.transpose(0, 2, 1), kc[:, -keep:], vc[:, -keep:]

def causal_dwconv(u_ext, conv_w, conv_b):
    y = lax.conv_general_dilated(
        u_ext, conv_w[:, None, :], window_strides=(1,), padding='VALID',
        dimension_numbers=('NWC', 'WIO', 'NWC'), feature_group_count=CONV_CH)
    return y + conv_b

def mixer_outputs(x, attn_outs, attn_lses, u_ext, gates, conv_w, conv_b, conv_ln_g, conv_ln_b,
                  w_attn_out, w_conv_out, w_o, norm2_g, w_ff1, w_ff2):
    B, T, _ = x.shape
    alpha = jax.nn.softmax(jnp.stack(attn_lses, axis=0), axis=0)
    o = jnp.einsum('gbth,gbthe->bthe', alpha, jnp.stack(attn_outs, axis=0)).astype(x.dtype)
    a = o.reshape(B, T, ATTN_WIDTH) @ w_attn_out
    c = causal_dwconv(u_ext, conv_w, conv_b)
    c = jax.nn.silu(layernorm(c, conv_ln_g, conv_ln_b)) @ w_conv_out
    g_a, g_c = jnp.split(gates, 2, axis=-1)
    merged = jax.nn.sigmoid(g_a) * a + jax.nn.sigmoid(g_c) * c
    h = x + merged @ w_o
    hn = rmsnorm(h, norm2_g)
    return h + jnp.square(jax.nn.relu(hn @ w_ff1)) @ w_ff2

def setup_inputs(seed: int = 0) -> dict:
    key = jax.random.key(seed)
    ks = jax.random.split(key, 24)
    f32 = jnp.float32
    nrm = lambda k, shape, scale: jax.random.normal(k, shape, f32) * scale
    inp = {}
    inp['x_prompt'] = nrm(ks[0], (BATCH, SEQ, D_MODEL), 1.0)
    inp['x_sample'] = nrm(ks[1], (DEC_BATCH, DEC_SEQ, D_MODEL), 1.0)
    for g in range(N_GROUPS):
        lb = min(GROUP_WINDOWS[g], PAST_LEN)
        shape = (DEPTH, DEC_BATCH, lb, HEADS_PER_GROUP, HEAD_DIM)
        inp['cache_k%d' % (g + 1)] = nrm(ks[2 + 2 * g], shape, 1.0)
        inp['cache_v%d' % (g + 1)] = nrm(ks[3 + 2 * g], shape, 1.0)
    inp['state_conv'] = nrm(ks[8], (DEPTH, DEC_BATCH, CONV_WIDTH - 1, CONV_CH), 0.5)
    inp['norm1_g'] = 1.0 + nrm(ks[9], (DEPTH, D_MODEL), 0.05)
    inp['w_in'] = nrm(ks[10], (DEPTH, D_MODEL, IN_WIDTH), D_MODEL ** -0.5)
    inp['q_norm_g'] = 1.0 + nrm(ks[11], (DEPTH, N_GROUPS, HEAD_DIM), 0.05)
    inp['k_norm_g'] = 1.0 + nrm(ks[12], (DEPTH, N_GROUPS, HEAD_DIM), 0.05)
    inp['conv_w'] = nrm(ks[13], (DEPTH, CONV_WIDTH, CONV_CH), CONV_WIDTH ** -0.5)
    inp['conv_b'] = nrm(ks[14], (DEPTH, CONV_CH), 0.01)
    inp['conv_ln_g'] = 1.0 + nrm(ks[15], (DEPTH, CONV_CH), 0.05)
    inp['conv_ln_b'] = nrm(ks[16], (DEPTH, CONV_CH), 0.01)
    inp['w_attn_out'] = nrm(ks[17], (DEPTH, ATTN_WIDTH, D_MODEL), ATTN_WIDTH ** -0.5)
    inp['w_conv_out'] = nrm(ks[18], (DEPTH, CONV_CH, D_MODEL), CONV_CH ** -0.5)
    inp['w_o'] = nrm(ks[19], (DEPTH, D_MODEL, D_MODEL), D_MODEL ** -0.5)
    inp['norm2_g'] = 1.0 + nrm(ks[20], (DEPTH, D_MODEL), 0.05)
    inp['w_ff1'] = nrm(ks[21], (DEPTH, D_MODEL, D_FF), D_MODEL ** -0.5)
    inp['w_ff2'] = nrm(ks[22], (DEPTH, D_FF, D_MODEL), D_FF ** -0.5)
    return inp

def reference(x_prompt, x_sample, cache_k1, cache_v1, cache_k2, cache_v2, cache_k3, cache_v3,
              state_conv, norm1_g, w_in, q_norm_g, k_norm_g, conv_w, conv_b, conv_ln_g, conv_ln_b,
              w_attn_out, w_conv_out, w_o, norm2_g, w_ff1, w_ff2):
    cache_k = (cache_k1, cache_k2, cache_k3)
    cache_v = (cache_v1, cache_v2, cache_v3)
    pk = [[] for _ in range(N_GROUPS)]
    pv = [[] for _ in range(N_GROUPS)]
    sk = [[] for _ in range(N_GROUPS)]
    sv = [[] for _ in range(N_GROUPS)]
    p_conv, s_conv = [], []
    xp, xs = x_prompt, x_sample
    for l in range(DEPTH):
        out_w = (conv_w[l], conv_b[l], conv_ln_g[l], conv_ln_b[l], w_attn_out[l], w_conv_out[l],
                 w_o[l], norm2_g[l], w_ff1[l], w_ff2[l])
        q, k, v, u, gates = mixer_inputs(xp, norm1_g[l], w_in[l], q_norm_g[l], k_norm_g[l])
        outs, lses = [], []
        for g in range(N_GROUPS):
            o, lse = dilated_attention_prompt(q[:, :, g], k[:, :, g], v[:, :, g],
                                              GROUP_DILATIONS[g], GROUP_WINDOWS[g])
            outs.append(o)
            lses.append(lse)
            keep = min(GROUP_WINDOWS[g], xp.shape[1])
            pk[g].append(k[:, -keep:, g])
            pv[g].append(v[:, -keep:, g])
        u_ext = jnp.pad(u, ((0, 0), (CONV_WIDTH - 1, 0), (0, 0)))
        p_conv.append(u_ext[:, -(CONV_WIDTH - 1):])
        xp = mixer_outputs(xp, outs, lses, u_ext, gates, *out_w)
        q, k, v, u, gates = mixer_inputs(xs, norm1_g[l], w_in[l], q_norm_g[l], k_norm_g[l])
        outs, lses = [], []
        for g in range(N_GROUPS):
            o, lse, nk, nv = dilated_attention_sample(q[:, :, g], k[:, :, g], v[:, :, g],
                                                      cache_k[g][l], cache_v[g][l],
                                                      GROUP_DILATIONS[g], GROUP_WINDOWS[g])
            outs.append(o)
            lses.append(lse)
            sk[g].append(nk)
            sv[g].append(nv)
        u_ext = jnp.concatenate([state_conv[l], u], axis=1)
        s_conv.append(u_ext[:, -(CONV_WIDTH - 1):])
        xs = mixer_outputs(xs, outs, lses, u_ext, gates, *out_w)
    st = lambda lst: jnp.stack(lst, axis=0)
    return (xp, xs,
            st(pk[0]), st(pv[0]), st(pk[1]), st(pv[1]), st(pk[2]), st(pv[2]), st(p_conv),
            st(sk[0]), st(sv[0]), st(sk[1]), st(sv[1]), st(sk[2]), st(sv[2]), st(s_conv))


_drawn_inputs = setup_inputs


def setup_inputs(seed=0):
    import zlib

    import numpy as np

    out = dict(_drawn_inputs(seed))
    spreads = {}
    factors = {'q_norm_g': 8.0, 'conv_b': 8.0, 'conv_ln_g': 2.84, 'conv_ln_b': 8.0}
    for name, (base, spread) in spreads.items():
        noise = np.random.default_rng([zlib.crc32(name.encode()), seed]).standard_normal(out[name].shape)
        drawn = base * np.exp(spread * noise) if base else spread * noise
        out[name] = __import__('jax').numpy.asarray(drawn.astype(out[name].dtype))
    for name, factor in factors.items():
        out[name] = (out[name] * factor).astype(out[name].dtype)
    return out
```

```python
from contextlib import ExitStack

import concourse.bass as bass
from concourse import mybir

F32 = mybir.dt.float32
F32R = mybir.dt.float32r
I32 = mybir.dt.int32
ALU = mybir.AluOpType
ACT = mybir.ActivationFunctionType
AX = mybir.AxisListType

P = 128
D = 1024
KT = D // P
TP = 512
NB = TP // P
TS = 8
T = TP + TS
HT = T // 2
G = 3
HEADS = 8
E = 64
AW = HEADS * E
CW = 31
DFF = 4096
EPS = 1e-6
NEG = -1e30
LOWEST = -3e38
DIL = (1, 4, 16)
CACHE = (128, 512, 1024)
SROWS = (128, 128, 67)
SKEYS = sum(SROWS)

COL_Q, COL_K, COL_V = 0, G * AW, 2 * G * AW
COL_GA = 3 * G * AW
COL_GB = COL_GA + D
COL_GATE_A = COL_GB + D
COL_GATE_C = COL_GATE_A + D

U_GLU = 0
U_QKV = U_GLU + 16
PER_T = 9 + 2
U_CGATE = U_QKV + 4 * PER_T
U_COUT = U_CGATE + 8
U_AOUT = U_COUT + 8
U_WO = U_AOUT + 4
U_FF = U_WO + 8
UNITS = U_FF + 64

GLU_TAPS = 8
SLOT_TAPS = 3
TB_PER_T = 38


def conv_schedule():
    taps = [(tile, tap) for tap in range(GLU_TAPS, CW) for tile in range(2)]
    cuts, at = [], 0
    for slot in range(17):
        n = 2 if slot == 0 else 3
        cuts.append(taps[at:at + n])
        at += n
    assert at >= len(taps)
    return cuts


def build_step(nc, x_prompt, x_sample, cache_k1, cache_v1, cache_k2, cache_v2, cache_k3, cache_v3,
               state_conv, norm1_g, w_in, q_norm_g, k_norm_g, conv_w, conv_b, conv_ln_g, conv_ln_b,
               w_attn_out, w_conv_out, w_o, norm2_g, w_ff1, w_ff2,
               y_prompt, y_sample, pk1, pv1, pk2, pv2, pk3, pv3, p_conv,
               sk1, sv1, sk2, sv2, sk3, sv3, s_conv):
    cache_k, cache_v = (cache_k1, cache_k2, cache_k3), (cache_v1, cache_v2, cache_v3)
    pk, pv = (pk1, pk2, pk3), (pv1, pv2, pv3)
    sk, sv = (sk1, sk2, sk3), (sv1, sv2, sv3)

    def rows(a):
        return a[0].rearrange("b r h e -> b r (h e)")

    ctx = ExitStack()
    with ctx:
        def sem(name):
            return ctx.enter_context(nc.semaphore(name))

        BASE = 16512

        def place(name, shape, dt, at):
            size = 4
            for n in shape[1:]:
                size *= n
            at = (at + 31) // 32 * 32
            return nc.alloc_sbuf_tensor_at(name, shape, dt, offset=BASE + at), at + size

        pos = 0
        x_high, pos = place("x_high", [P, KT, T], F32R, pos)
        x_low, pos = place("x_low", [P, KT, T], F32R, pos)
        w_raw0, pos = place("w_raw0", [P, KT, P], F32, pos)
        w_raw1, pos = place("w_raw1", [P, KT, P], F32, pos)
        w_high0, pos = place("w_high0", [P, KT, P], F32R, pos)
        w_high1, pos = place("w_high1", [P, KT, P], F32R, pos)
        w_low0, pos = place("w_low0", [P, KT, P], F32R, pos)
        w_low1, pos = place("w_low1", [P, KT, P], F32R, pos)
        w_raw, w_high, w_low = (w_raw0, w_raw1), (w_high0, w_high1), (w_low0, w_low1)
        ident, pos = place("ident", [P, P], F32, pos)
        ones, pos = place("ones", [P, P], F32, pos)
        head_ones, pos = place("head_ones", [P, P], F32, pos)
        mask, pos = place("mask", [P, G, TP], F32, pos)
        dist, pos = place("dist", [P, P], I32, pos)
        dist_mod, pos = place("dist_mod", [P, P], I32, pos)
        mod_mask, pos = place("mod_mask", [P, P], F32, pos)
        qk_gain, pos = place("qk_gain", [P, 6], F32, pos)
        NCV = CW + 4
        chan, pos = place("chan", [P, KT, NCV], F32, pos)
        C_BIAS, C_LNG, C_LNB, C_N2 = CW, CW + 1, CW + 2, CW + 3
        eps_col, pos = place("eps_col", [P, 1], F32, pos)
        credit, pos = place("credit", [P, 8], F32, pos)
        s_small, pos = place("s_small", [P, 16], F32, pos)
        pool_mark, pos = place("pool_mark", [P, 1], F32, pos)
        x_ss, pos = place("x_ss", [P, 5], F32, pos)
        x_rstd, pos = place("x_rstd", [P, 5], F32, pos)
        job_max, pos = place("job_max", [P, 2, 4], F32, pos)
        job_sum, pos = place("job_sum", [P, 2, 4], F32, pos)
        pos = (pos + 31) // 32 * 32
        UW = CW - 1 + T
        U0 = pos
        u_in, pos = place("u_in", [P, KT, UW], F32, pos)
        conv, pos = place("conv", [P, KT, T], F32, pos)
        attn, pos = place("attn", [P, 4, T], F32, pos)
        QR = pos
        at = QR
        x_tok, at = place("x_tok", [P, 5, D], F32, at)
        gain1, at = place("gain1", [P, D], F32, at)
        junk, at = place("junk", [P, D], F32, at)
        xn_tok, at = place("xn_tok", [P, 2, D], F32, at)
        chan_rows, at = place("chan_rows", [NCV, D], F32, at)
        state_rows, at = place("state_rows", [120, 2, D], F32, at)
        at = QR
        qk, at = place("qk", [P, 6, T], F32, at)
        square, at = place("square", [P, 2, T], F32, at)
        rstd, at = place("rstd", [P, 2, T], F32, at)
        v_feat, at = place("v_feat", [P, G, T], F32, at)
        k_tok, at = place("k_tok", [P, NB, G, P], F32, at)
        v_tok, at = place("v_tok", [P, NB, G, P], F32, at)
        new_tok, at = place("new_tok", [TS, 3, G, P], F32, at)
        probs, at = place("probs", [P, 2, 1280], F32, at)
        probs_t, at = place("probs_t", [P, 2, 1280], F32, at)
        o_tok, at = place("o_tok", [P, NB, P], F32, at)
        glu_sig, at = place("glu_sig", [P, 2, T], F32, at)
        gate_stage = glu_sig
        GEND = at
        state, at = place("state", [P, KT, TS, CW - 1], F32, at)
        assert at <= 212863 - 64, at
        c_high, _ = place("c_high", [P, KT, T], F32R, U0)
        at = QR
        c_low, at = place("c_low", [P, KT, T], F32R, at)
        KB = at
        kbuf, at = place("kbuf", [P, TS, AW], F32, at)
        qbuf, at = place("qbuf", [P, TS, AW], F32, at)
        _, at2 = place("x_tok2_", [P, 5, D], F32, KB)
        x_tok2 = nc.alloc_sbuf_tensor_at("x_tok2", [P, 5, D], F32, offset=BASE + KB)
        x_feat, at2 = place("x_feat", [P, KT, T], F32, at2)
        at = max(at, at2)
        gate_c, at = place("gate_c", [P, KT, T], F32, at)
        h_feat = nc.alloc_sbuf_tensor_at("h_feat", [P, KT, T], F32, offset=BASE + at - 4 * KT * T)
        GA = at
        gate_a, at = place("gate_a", [P, KT, T], F32, at)
        s_score, at = place("s_score", [P, G, TS * HEADS], F32, at)
        s_prob, at = place("s_prob", [TS * HEADS, SKEYS], F32, at)
        s_prob_t, at = place("s_prob_t", [P, G, TS * HEADS], F32, at)
        SMALL = at
        assert at <= 212863 - 64, at
        kbuf2, _ = place("kbuf2", [P, TS, AW], F32, GA)
        at = QR + 4 * T * 5
        ln_sq, at = place("ln_sq", [P, 2, T], F32, at)
        ln_sum, at = place("ln_sum", [P, T], F32, at)
        at = SMALL
        ln_rstd, at = place("ln_rstd", [P, T], F32, at)
        c_sum, at = place("c_sum", [P, T], F32, at)
        state_out, at = place("state_out", [CW - 1 + TS, D], F32, at)
        assert at <= 212863 - 64, at
        o_high = nc.alloc_sbuf_tensor_at("o_high", [P, 4, T], F32R, offset=BASE + U0 + 4 * KT * UW)
        o_low = nc.alloc_sbuf_tensor_at("o_low", [P, 4, T], F32R, offset=BASE + U0 + 4 * KT * UW + 16 * T)
        at = GA
        h_sq, at = place("h_sq", [P, 2, T], F32, at)
        h_ss, at = place("h_ss", [P, T], F32, at)
        h_rs2, at = place("h_rs2", [P, T], F32, at)
        relu, at = place("relu", [P, 2, T], F32, at)
        hid, at = place("hid", [P, 2, T], F32, at)
        assert at <= 212863 - 64, at
        hid_high, at = place("hid_high", [P, 16, T], F32R, U0)
        hid_low, at = place("hid_low", [P, 16, T], F32R, at)
        assert at <= GA - 4 * KT * T, (at, GA)
        y_feat, at = place("y_feat", [P, 2, T], F32, GA + 4 * T * 8)
        y_tok, at = place("y_tok", [P, 2, NB, P], F32, at)
        ys_tok, at = place("ys_tok", [TS, 2, P], F32, at)
        assert at <= 212863 - 64, at

        ps = ctx.enter_context(nc.psum_tensor("ps", [P, 8, 512], F32))

        def pair(n):
            return ps[:, 2 * n:2 * n + 2, 0:HT]

        def halves(a):
            return a.rearrange("p (h c) -> p h c", h=2)

        gate_rows = nc.dram_tensor("gate_rows", [P, KT, T], F32).ap()
        scratch = nc.dram_tensor("new_qkv", [3, TS, G, AW], F32).ap()

        raw_full = [sem("raw_full0"), sem("raw_full1")]
        cast_done = sem("cast_done")
        split_done = sem("split_done")
        unit_done = sem("unit_done")
        tile_free = sem("tile_free")
        x_in = sem("x_in")
        gain_in = sem("gain_in")
        chan_in = sem("chan_in")
        state_in = sem("state_in")
        qkg_in = sem("qkg_in")
        consts = sem("consts")
        pool_c = sem("pool_c")
        dve_c = sem("dve_c")
        mask_done = sem("mask_done")
        x_sq = sem("x_sq")
        x_var = sem("x_var")
        x_sd = sem("x_sd")
        x_rs = sem("x_rs")
        x_scaled = sem("x_scaled")
        x_tr = sem("x_tr")
        x_high_done = sem("x_high_done")
        x_low_done = sem("x_low_done")
        chan_tr = sem("chan_tr")
        chan_done = sem("chan_done")
        state_tr = sem("state_tr")
        state_done = sem("state_done")
        glu_sig_done = sem("glu_sig_done")
        u_done = sem("u_done")
        tap_done = sem("tap_done")
        sconv = sem("sconv")
        sq_done = sem("sq_done")
        tb_full = sem("tb_full")
        tb_free = sem("tb_free")
        rs_done = sem("rs_done")
        norm_done = sem("norm_done")
        v_done = sem("v_done")
        scores = sem("scores")
        masked = sem("masked")
        max_done = sem("max_done")
        exp_done = sem("exp_done")
        sum_done = sem("sum_done")
        rsum_done = sem("rsum_done")
        o_done = sem("o_done")
        o_norm = sem("o_norm")
        kv_stored = sem("kv_stored")
        new_stored = sem("new_stored")
        rows_free = sem("rows_free")
        c_summed = sem("c_summed")
        mean_done = sem("mean_done")
        centred = sem("centred")
        csq_done = sem("csq_done")
        csq_sum = sem("csq_sum")
        var_done = sem("var_done")
        ln_sd = sem("ln_sd")
        ln_rs = sem("ln_rs")
        ln_scaled = sem("ln_scaled")
        silu_done = sem("silu_done")
        c_high_done = sem("c_high_done")
        c_low_done = sem("c_low_done")
        ut_done = sem("ut_done")
        ut_copied = sem("ut_copied")
        gate_copied = sem("gate_copied")
        gates_stored = sem("gates_stored")
        gates_in = sem("gates_in")
        agate_done = sem("agate_done")
        abranch = sem("abranch")
        merged = sem("merged")
        m_high = sem("m_high")
        m_low = sem("m_low")
        o_high_done = sem("o_high_done")
        o_low_done = sem("o_low_done")
        k_in = sem("k_in")
        q_in = sem("q_in")
        kn_in = sem("kn_in")
        qn_in = sem("qn_in")
        kq_done = sem("kq_done")
        s_red = sem("s_red")
        s_tr = sem("s_tr")
        s_mx = sem("s_mx")
        s_exp = sem("s_exp")
        s_rs = sem("s_rs")
        s_pn = sem("s_pn")
        s_ptr = sem("s_ptr")
        s_ptc = sem("s_ptc")
        v_in = [sem("v_in0"), sem("v_in1"), sem("v_in2")]
        vn_in = sem("vn_in")
        s_pv = sem("s_pv")
        s_out = sem("s_out")
        x2_in = sem("x2_in")
        xt_full = sem("xt_full")
        xt_copied = sem("xt_copied")
        hsq_done = sem("hsq_done")
        hss_sum = sem("hss_sum")
        hss_done = sem("hss_done")
        h_rs = sem("h_rs")
        hn_high = sem("hn_high")
        hn_low = sem("hn_low")
        relu_done = sem("relu_done")
        rsq_done = sem("rsq_done")
        hid_done = sem("hid_done")
        hid_hi = sem("hid_hi")
        hid_lo = sem("hid_lo")
        y_tr = sem("y_tr")
        y_copied = sem("y_copied")
        y_half = sem("y_half")
        y_out = [sem("y_out0"), sem("y_out1")]
        copies = sem("copies")
        conv_out = sem("conv_out")
        new_rows = sem("new_rows")

        win = w_in[0].rearrange("(k p) n -> p k n", p=P)
        wao = w_attn_out[0].rearrange("(k p) n -> p k n", p=P)
        wco = w_conv_out[0].rearrange("(k p) n -> p k n", p=P)
        wo = w_o[0].rearrange("(k p) n -> p k n", p=P)
        wf1 = w_ff1[0].rearrange("(k p) n -> p k n", p=P)
        wf2 = w_ff2[0].rearrange("(q k p) n -> q p k n", q=4, p=P)

        block = ctx.enter_context(nc.Block())

        @block.sync
        def _(sp):
            sp.dma_start(x_tok[:, 0:NB, :], x_prompt[0].rearrange("(b p) d -> p b d", p=P)).then_inc(x_in, 16)
            sp.dma_start(x_tok[0:TS, NB, :], x_sample.rearrange("b s d -> (b s) d")).then_inc(x_in, 16)
            sp.dma_start(gain1[:, :], norm1_g.to_broadcast([P, D])).then_inc(gain_in, 16)

            def load(a, b, it, src, dst=None):
                sp.wait_ge(split_done, at_(a + 1, b, it))
                sp.dma_start(w_raw[a % 2][:, :, :] if dst is None else dst, src).then_inc(raw_full[a % 2], 16)

            def copy_rows(g, which, b):
                src = rows((cache_k, cache_v)[which][g])
                dst = rows((sk, sv)[which][g])
                n = CACHE[g] - 1 if g < 2 else CACHE[g]
                skip = CACHE[g] - n
                sp.dma_start(dst[bass.ds(b, 1), 0:n, :], src[bass.ds(b, 1), skip:skip + n, :]).then_inc(copies, 16)

            for u in range(2):
                load(u, 0, 0, win[:, :, COL_GA + u * D:COL_GA + u * D + P])
            sp.dma_start(chan_rows[0:CW, :], conv_w[0]).then_inc(chan_in, 16)
            for r, vec in ((C_BIAS, conv_b), (C_LNG, conv_ln_g), (C_LNB, conv_ln_b), (C_N2, norm2_g)):
                sp.dma_start(chan_rows[r:r + 1, :], vec).then_inc(chan_in, 16)
            sp.dma_start(state_rows[:, :, :], state_conv[0].rearrange("(h b) r c -> (b r) h c", h=2)).then_inc(state_in, 16)
            for u in range(2, 4):
                load(u, 0, 0, win[:, :, COL_GA + (u % 2) * D + P:COL_GA + (u % 2) * D + 2 * P])
            with sp.Fori(1, 4) as it:
                for j in range(4):
                    load(U_GLU + j, 4, it, win[:, :, bass.ds(it * 2 * P + COL_GA + (j % 2) * D + (j // 2) * P, P)])
            with sp.Fori(0, 2) as tt:
                for t2 in range(2):
                    for i in range(9):
                        col = (i // G) * G * AW + (i % G) * AW + t2 * P
                        load(U_QKV + PER_T * t2 + i, 2 * PER_T, tt, win[:, :, bass.ds(tt * 2 * P + col, P)])
                        if i < 8:
                            copy_rows(i // 4, i // 2 % 2, tt * 4 + 2 * t2 + i % 2)
                        else:
                            copy_rows(2, 1, tt * 4 + 2 * t2)
                            copy_rows(2, 1, tt * 4 + 2 * t2 + 1)
                    for i in range(2):
                        load(U_QKV + PER_T * t2 + 9 + i, 2 * PER_T, tt,
                             win[:, :, bass.ds(tt * 4 * P + COL_GATE_A + (2 * t2 + i) * P, P)])
            with sp.Fori(0, 2) as it:
                for j in range(4):
                    load(U_CGATE + j, 4, it, win[:, :, bass.ds(it * 4 * P + COL_GATE_C + j * P, P)])
            with sp.Fori(0, 2) as it:
                for j in range(4):
                    load(U_COUT + j, 4, it, wco[:, :, bass.ds(it * 4 * P + j * P, P)])
            with sp.Fori(0, 2) as it:
                for j in range(2):
                    load(U_AOUT + j, 2, it, wao[:, :, bass.ds(it * 4 * P + j * 2 * P, 2 * P)],
                         w_raw[j][:, :, :].rearrange("p k n -> p (k n)").rearrange("p (k n) -> p k n", k=4))
            with sp.Fori(0, 2) as it:
                for j in range(4):
                    load(U_WO + j, 4, it, wo[:, :, bass.ds(it * 4 * P + j * P, P)])
            for c in range(2):
                with sp.Fori(0, 4) as it:
                    for j in range(4):
                        load(U_FF + 32 * c + j, 4, it, wf1[:, :, bass.ds(it * 4 * P + 16 * c * P + j * P, P)])
                    copy_rows(2, 0, it + 4 * c)
                with sp.Fori(0, 4) as it:
                    for j in range(4):
                        load(U_FF + 32 * c + 16 + j, 4, it,
                             wf2[2 * c + j % 2][:, :, bass.ds(it * 2 * P + (j // 2) * P, P)])
            sp.wait_ge(copies, 16 * 48)
            sp.wait_ge(new_rows, 16 * 7)
            sp.wait_ge(conv_out, 16 * 2)
            sp.wait_ge(kv_stored, 16 * 6 * 4)
            sp.wait_ge(new_stored, 16 * 3 * 4)
            sp.wait_ge(gates_stored, 16 * 4)
            for slot in range(2):
                sp.wait_ge(y_out[slot], 16 * 2 * 4)

        def qkv_pair(pe, unit, tt, t2):
            def cnt(per_t, n):
                return at_(per_t * t2 + n, 2 * per_t, tt)

            tb = [0]

            def bank():
                n = tb[0]
                tb[0] += 1
                pe.wait_ge(tb_free, cnt(TB_PER_T, n + 1))
                return 6 + n % 2

            def project(i):
                if i < 2:
                    pe.wait_ge(o_norm, cnt(8, 2))
                elif i == 2:
                    pe.wait_ge(gate_copied, cnt(2, 2))
                else:
                    pe.wait_ge(norm_done, cnt(6, i - 2))
                unit(U_QKV + PER_T * t2 + i, 2 * PER_T, tt, pair(i % 3), x_high, x_low).then_inc(unit_done, 1)

            def gate_part(j, second):
                k = 2 * (j % 4) + second
                if k == 0:
                    pe.wait_ge(gate_copied, cnt(2, j // 4 + 2))
                mm = unit(U_QKV + PER_T * t2 + 9 + j // 4, 2 * PER_T, tt, pair(2), x_high, x_low, part=k)
                if k == KT - 1:
                    mm.then_inc(unit_done, 1)

            def sums(i):
                pe.wait_ge(sq_done, cnt(6, i + 1))
                for h in range(2):
                    mm = pe.matmul(ps[:, bank(), 0:HT], head_ones[:, :], square[:, i % 2, h * HT:(h + 1) * HT], start=True, stop=True)
                mm.then_inc(tb_full, 2)

            def kv_transposes(src):
                nb = bank()
                for blk in range(NB):
                    mm = pe.transpose(ps[:, nb, blk * P:(blk + 1) * P], src[:, blk * P:(blk + 1) * P], ident[:, :])
                mm.then_inc(tb_full, 1)

            def new_transposes(srcs):
                nb = bank()
                for g in range(G):
                    mm = pe.transpose(ps[0:TS, nb, g * P:(g + 1) * P], srcs[:, g, TP:T], ident[:, :])
                mm.then_inc(tb_full, 1)

            def score(j):
                hh, b = j // 4, j % 4
                hp = slice(hh * E, (hh + 1) * E)
                if j:
                    pe.wait_ge(exp_done, cnt(8, j))
                for g in range(G):
                    k0 = (max(b - 1, 0) if g == 0 else 0) * P
                    n = (b + 1) * P - k0
                    mm = pe.matmul(ps[:, g, 512 - n:512], qk[hp, g, b * P:(b + 1) * P], qk[hp, 3 + g, k0:k0 + n], start=True, stop=True)
                mm.then_inc(scores, 1)

            def blocks(j):
                b = j % 4
                return [(0, kb) for kb in range(max(b - 1, 0), b + 1)] + [(g, kb) for g in (1, 2) for kb in range(b + 1)]

            tbp = [0]

            def attend(j):
                hh = j // 4
                bl = blocks(j)
                groups = [bl[i:i + 4] for i in range(0, len(bl), 4)]
                pe.wait_ge(exp_done, cnt(8, j + 1))

                def turn(gi):
                    nb = bank()
                    for n in range(len(groups[gi])):
                        c0 = (4 * gi + n) * P
                        mm = pe.transpose(ps[:, nb, n * P:(n + 1) * P], probs[:, j % 2, c0:c0 + P], ident[:, :])
                    mm.then_inc(tb_full, 1)

                base = tb[0]
                for gi in range(min(2, len(groups))):
                    turn(gi)
                gate_part(j, 0)
                pe.wait_ge(o_norm, cnt(8, j + 2))
                for gi in range(len(groups)):
                    pe.wait_ge(tb_free, cnt(TB_PER_T, base + gi + 1 + 2))
                    if gi + 2 < len(groups):
                        turn(gi + 2)
                    for n, (g, kb) in enumerate(groups[gi]):
                        c0 = (4 * gi + n) * P
                        mm = pe.matmul(ps[:, 3, 0:E], probs_t[:, j % 2, c0:c0 + P], v_tok[:, kb, g, hh * E:(hh + 1) * E],
                                       start=(gi == 0 and n == 0), stop=(4 * gi + n == len(bl) - 1))
                    if gi == 0 and len(groups) > 1:
                        gate_part(j, 1)
                mm.then_inc(o_done, 1)
                if len(groups) == 1:
                    gate_part(j, 1)

            for i in range(8):
                if i == 2:
                    pe.wait_ge(u_done, 8 + 2)
                project(i)
                if 1 <= i <= 6:
                    sums(i - 1)
            for i in (3, 4):
                if i == 3:
                    pe.wait_ge(norm_done, cnt(6, 5))
                kv_transposes(qk[:, i, :])
            project(8)
            pe.wait_ge(norm_done, cnt(6, 6))
            kv_transposes(qk[:, 5, :])
            pe.wait_ge(v_done, cnt(3, 2))
            score(0)
            kv_transposes(v_feat[:, 0, :])
            kv_transposes(v_feat[:, 1, :])
            new_transposes(qk[:, 0:G, :])
            pe.wait_ge(v_done, cnt(3, 3))
            kv_transposes(v_feat[:, 2, :])
            new_transposes(qk[:, G:2 * G, :])
            new_transposes(v_feat[:, :, :])
            pe.wait_ge(tb_free, cnt(TB_PER_T, 19 + 2))
            for j in range(8):
                if j < 7:
                    score(j + 1)
                attend(j)
            pe.wait_ge(o_norm, cnt(8, 8 + 2))
            nb = bank()
            for b in range(NB):
                mm = pe.transpose(ps[:, nb, b * P:(b + 1) * P], o_tok[:, b, :], ident[:, :])
            mm.then_inc(tb_full, 1)
            assert tb[0] == TB_PER_T, tb


        @block.tensor
        def _(pe):
            def unit(a, b, it, out, high, low, ready=None, k0=0, first=True, last=True, cols=None, part=None):
                if not part:
                    pe.wait_ge(split_done, at_(a + 1 + 2, b, it))
                wh, wl = w_high[a % 2], w_low[a % 2]
                nk = KT
                if cols is not None:
                    nk = 4
                    wh = wh[:, :, :].rearrange("p k n -> p (k n)").rearrange("p (k n) -> p k n", k=4)
                    wl = wl[:, :, :].rearrange("p k n -> p (k n)").rearrange("p (k n) -> p k n", k=4)
                for k in (range(nk) if part is None else (part,)):
                    if ready is not None:
                        ready(k)
                    n0 = 0 if cols is None else cols
                    for n, (w, x) in enumerate(((wh, high), (wh, low), (wl, high))):
                        for h in range(2):
                            mm = pe.matmul(out[:, h, :], w[:, k, n0:n0 + P], x[:, k0 + k, h * HT:(h + 1) * HT],
                                           start=(first and k == 0 and n == 0), stop=(last and k == nk - 1 and n == 2))
                return mm

            pe.wait_ge(consts, 1)
            pe.wait_ge(chan_in, 16 * 5)
            for k in range(KT):
                mm = pe.transpose(ps[:, 3, k * NCV:(k + 1) * NCV], chan_rows[:, k * P:(k + 1) * P], ident[0:NCV, 0:NCV])
            mm.then_inc(chan_tr, 1)
            for i in range(5):
                n = P if i < NB else TS
                pe.wait_ge(x_scaled, i + 1)
                if i == 1:
                    pe.wait_ge(chan_done, 1)
                if i >= 2:
                    pe.wait_ge(x_low_done, i - 1)
                for k in range(KT):
                    mm = pe.transpose(ps[:, 2 * (i % 2) + k // 4, (k % 4) * P:(k % 4) * P + n],
                                      xn_tok[0:n, i % 2, k * P:(k + 1) * P], ident[0:n, 0:n])
                mm.then_inc(x_tr, 1)
            pe.wait_ge(state_in, 16)
            for k in range(KT):
                for h in range(2):
                    mm = pe.transpose(ps[:, 4 + k // 2, (k % 2) * 240 + h * 120:(k % 2) * 240 + (h + 1) * 120],
                                      state_rows[:, h, k * P:(k + 1) * P], ident[0:120, 0:120])
            mm.then_inc(state_tr, 1)
            pe.wait_ge(x_low_done, 5)
            pe.wait_ge(state_done, 1)

            with pe.Fori(0, 4) as it:
                for j in range(4):
                    pe.wait_ge(u_done, at_(j // 2 + 1, 2, it))
                    unit(U_GLU + j, 4, it, pair(j), x_high, x_low).then_inc(unit_done, 1)
            pe.wait_ge(u_done, 7 + 2)
            pe.wait_ge(pool_c, 7)

            with pe.Fori(0, 2) as tt:
                for t2 in range(2):
                    qkv_pair(pe, unit, tt, t2)
            pe.wait_ge(o_norm, 2 + 32)

            def tile(n, b, it):
                pe.wait_ge(tile_free, at_(n + 1, b, it))
                return pair(n % 2)

            for j in range(8):
                unit(U_CGATE + j, 0, 0, tile(j, 0, 0), x_high, x_low).then_inc(unit_done, 1)
                if j == 1:
                    pe.wait_ge(c_summed, KT)
                    for h in range(2):
                        mm = pe.matmul(ps[:, 4 + h, 0:HT], ones[:, :], c_sum[:, h * HT:(h + 1) * HT], start=True, stop=True)
                    mm.then_inc(mean_done, 1)
                if j == 2:
                    pe.wait_ge(tb_free, 2 + 4 * TB_PER_T)
                    for k in range(KT):
                        mm = pe.transpose(ps[0:CW - 1 + TS, 6 + k // 4, (k % 4) * P:(k % 4 + 1) * P],
                                          u_in[:, k, TP:UW], ident[:, :])
                    mm.then_inc(ut_done, 1)
                if j == 4:
                    pe.wait_ge(csq_sum, KT)
                    pe.wait_ge(ut_copied, 1)
                    for h in range(2):
                        mm = pe.matmul(ps[:, 6 + h, 0:HT], ones[:, :], ln_sum[:, h * HT:(h + 1) * HT], start=True, stop=True)
                    mm.then_inc(var_done, 1)
            def sample_values(g):
                n = SROWS[g]
                vbuf = (kbuf2, qbuf, kbuf)[g]
                pe.wait_ge(v_in[g], 16)
                if g == 2:
                    pe.wait_ge(vn_in, 16)
                for b in range(TS):
                    for ct in range(4):
                        mm = pe.matmul(ps[:, 6, (ct * TS + b) * 2:(ct * TS + b) * 2 + 2],
                                       vbuf[0:n, b, ct * P:(ct + 1) * P], s_prob_t[0:n, g, b * 8 + 2 * ct:b * 8 + 2 * ct + 2],
                                       start=(g == 0 and b == 0 and ct == 0), stop=(g == 2), skip_group_check=True)
                mm.then_inc(s_pv, 1)

            for j in range(8):
                unit(U_COUT + j, 0, 0, tile(8 + j, 0, 0), c_high, c_low,
                     ready=(lambda k: pe.wait_ge(c_low_done, k + 1)) if j == 0 else None).then_inc(unit_done, 1)
                if j == 5:
                    pe.wait_ge(s_red, 3)
                    pe.wait_ge(centred, KT)
                    at = 0
                    for g in range(G):
                        n = SROWS[g]
                        mm = pe.transpose(ps[0:64, 4, at:at + n], s_score[0:n, g, :], ident[0:n, 0:n])
                        at += n
                    mm.then_inc(s_tr, 1)
                if j == 6:
                    pe.wait_ge(s_pn, 1)
                    at = 0
                    for g in range(G):
                        n = SROWS[g]
                        mm = pe.transpose(ps[0:n, 5, g * 64:(g + 1) * 64], s_prob[:, at:at + n], ident[0:64, 0:64])
                        at += n
                    mm.then_inc(s_ptr, 1)
            pe.wait_ge(s_ptc, 2)
            pe.wait_ge(ln_rs, 1)
            for g in range(G):
                sample_values(g)
            with pe.Fori(0, 2) as it:
                for j in range(2):
                    for c in range(2):
                        mm = unit(U_AOUT + j, 2, it, tile(16 + 2 * j + c, 4, it), o_high, o_low, cols=c * P,
                                  ready=(lambda k: pe.wait_ge(o_low_done, 2)) if j == 0 and c == 0 else None)
                    mm.then_inc(unit_done, 1)
            pe.wait_ge(x2_in, 32)
            pe.wait_ge(s_out, 2)
            for k in range(KT):
                if k >= 3:
                    pe.wait_ge(xt_copied, k - 2)
                for b in range(NB):
                    mm = pe.transpose(ps[:, 4 + k % 3, b * P:(b + 1) * P], x_tok2[:, b, k * P:(k + 1) * P], ident[:, :])
                mm.then_inc(xt_full, 1)
            for k in range(KT):
                mm = pe.transpose(ps[:, 7, k * TS:(k + 1) * TS], x_tok2[0:TS, NB, k * P:(k + 1) * P], ident[0:TS, 0:TS])
            mm.then_inc(xt_full, 1)
            with pe.Fori(0, 2) as it:
                for j in range(4):
                    unit(U_WO + j, 4, it, tile(24 + j, 4, it), c_high, c_low,
                         ready=(lambda k: pe.wait_ge(m_low, k + 1)) if j == 0 else None).then_inc(unit_done, 1)

            for c in range(2):
                base = U_FF + 32 * c
                tiles = 32 + 24 * c
                if c == 0:
                    for j in range(4):
                        unit(base + j, 0, 0, tile(tiles + j, 0, 0), x_high, x_low,
                             ready=(lambda k: pe.wait_ge(hn_low, k + 1)) if j == 0 else None).then_inc(unit_done, 1)
                        if j == 0:
                            pe.wait_ge(hss_sum, KT + 2)
                            pe.wait_ge(xt_copied, KT + 1)
                            for h in range(2):
                                mm = pe.matmul(ps[:, 4 + h, 0:HT], ones[:, :], h_ss[:, h * HT:(h + 1) * HT], start=True, stop=True)
                            mm.then_inc(hss_done, 1)
                with pe.Fori(1 - c, 4) as it:
                    for j in range(4):
                        unit(base + j, 4, it, tile(tiles + j, 4, it), x_high, x_low).then_inc(unit_done, 1)
                def ff2(it, peeled=False):
                    for j in range(4):
                        n = j // 2
                        if j % 2 == 0:
                            out = tile(tiles + 16 + n, 2, it)
                        mm = unit(base + 16 + j, 4, it, out, hid_high, hid_low, k0=8 * (j % 2), first=(j % 2 == 0), last=(j % 2 == 1),
                                  ready=(lambda k: pe.wait_ge(hid_lo, 16 * c + 8 * (j % 2) + k + 1)) if n == 0 else None)
                        mm.then_inc(unit_done, 1)

                def y_transposes(n, b, it):
                    pe.wait_ge(tile_free, at_(tiles + 16 + n + 1 + 2, b, it))
                    pe.wait_ge(y_copied, at_(n + 1, b, it))
                    for blk in range(NB):
                        pe.transpose(ps[:, 4 + n % 2, blk * P:(blk + 1) * P], y_feat[:, n % 2, blk * P:(blk + 1) * P], ident[:, :])
                    pe.transpose(ps[0:TS, 6 + n % 2, 0:P], y_feat[:, n % 2, TP:T], ident[:, :]).then_inc(y_tr, 1)

                if c == 0:
                    with pe.Fori(0, 4) as it:
                        ff2(it)
                else:
                    def ff2_last(b, it, with_prev):
                        for j in range(4):
                            n = j // 2
                            if j % 2 == 0:
                                out = tile(tiles + 16 + n, b, it)
                            mm = unit(base + 16 + j, 2 * b, it, out, hid_high, hid_low, k0=8 * (j % 2), first=(j % 2 == 0), last=(j % 2 == 1),
                                      ready=(lambda k: pe.wait_ge(hid_lo, 16 * c + 8 * (j % 2) + k + 1)) if n == 0 else None)
                            mm.then_inc(unit_done, 1)
                            if j == 2:
                                y_transposes(0, b, it)
                            if j == 0 and with_prev:
                                y_transposes(-1, b, it)
                    ff2_last(0, 0, False)
                    with pe.Fori(1, 4) as it:
                        ff2_last(2, it, True)
                    y_transposes(7, 0, 0)

        def ln_silu(act, k):
            act.wait_ge(ln_scaled, k + 1)
            act.activation(conv[:, k, :], conv[:, k, :], ACT.Silu, scale=chan[:, k, C_LNG:C_LNG + 1],
                           bias=chan[:, k, C_LNB:C_LNB + 1]).then_inc(silu_done, 1)
            act.wait_ge(silu_done, k + 1)
            act.activation(c_high[:, k, :], conv[:, k, :], ACT.Copy).then_inc(c_high_done, 1)

        def act_pair(act, cast, done, tt, t2):
            def cnt(per_t, n):
                return at_(per_t * t2 + n, 2 * per_t, tt)

            def next_cast(i):
                cast(U_QKV + PER_T * t2 + i + 2, 2 * PER_T, tt)

            tb = [0]

            def copy_bank(dst, np_, ncols, view=None):
                n = tb[0]
                tb[0] += 1
                act.wait_ge(tb_full, cnt(TB_PER_T, n + 1))
                src = ps[0:np_, 6 + n % 2, 0:ncols]
                if view:
                    src = src.rearrange("p (b c) -> p b c", c=P)
                return act.activation(dst, src, ACT.Copy)

            def root(i):
                tb[0] += 2
                act.wait_ge(tb_full, cnt(TB_PER_T, tb[0]))
                act.activation(halves(rstd[:, i % 2, :]), ps[:, 6:8, 0:HT], ACT.Ln, scale=1.0 / E, bias=eps_col[:, :]).then_inc(tb_free, 2)
                act.wait_ge(tb_free, cnt(TB_PER_T, tb[0] + 2))
                act.activation(rstd[:, i % 2, :], rstd[:, i % 2, :], ACT.Exp, scale=-0.5).then_inc(rs_done, 1)

            for i in range(9):
                next_cast(i)
                done(U_QKV + PER_T * t2 + i, 2 * PER_T, tt)
                if i < 6:
                    act.activation(halves(square[:, i % 2, :]), pair(i % 3), ACT.Square).then_inc(sq_done, 1)
                else:
                    act.activation(halves(v_feat[:, i - 6, :]), pair(i % 3), ACT.Copy).then_inc(v_done, 1)
                if 1 <= i <= 6:
                    if i >= 3:
                        act.wait_ge(norm_done, cnt(6, i - 2))
                    root(i - 1)
            act.wait_ge(rows_free, cnt(1, 1))
            copy_bank(k_tok[:, :, 0, :], P, 512, True).then_inc(tb_free, 1)
            copy_bank(k_tok[:, :, 1, :], P, 512, True).then_inc(tb_free, 1)
            copy_bank(k_tok[:, :, 2, :], P, 512, True).then_inc(tb_free, 1)
            copy_bank(v_tok[:, :, 0, :], P, 512, True).then_inc(tb_free, 1)
            copy_bank(v_tok[:, :, 1, :], P, 512, True).then_inc(tb_free, 1)
            copy_bank(new_tok[:, 0, :, :], TS, G * P, True).then_inc(tb_free, 1)
            copy_bank(v_tok[:, :, 2, :], P, 512, True).then_inc(tb_free, 1)
            copy_bank(new_tok[:, 1, :, :], TS, G * P, True).then_inc(tb_free, 1)
            copy_bank(new_tok[:, 2, :, :], TS, G * P, True).then_inc(tb_free, 1)

            def exponent(j):
                b = j % 4
                act.wait_ge(max_done, cnt(8, j + 1))
                at = 0
                for g in range(G):
                    n = (min(b, 1) + 1 if g == 0 else b + 1) * P
                    a = act.activation(probs[:, j % 2, at:at + n], ps[:, g, 512 - n:512], ACT.Exp,
                                       bias=job_max[:, j % 2, 3:4], accum_out=job_sum[:, j % 2, g:g + 1])
                    at += n
                a.then_inc(exp_done, 1)

            exponent(0)
            for j in range(8):
                b = j % 4
                n = (min(b, 1) + 1) + 2 * (b + 1)
                for c0 in range(0, n, 4):
                    m = min(4, n - c0)
                    copy_bank(probs_t[:, j % 2, c0 * P:(c0 + m) * P], P, m * P).then_inc(tb_free, 1)
                if j + 1 < 8:
                    exponent(j + 1)
                if j % 4 == 3:
                    next_cast(9 + j // 4)
                    act.activation(halves(gate_stage[:, j // 4, :]), pair(2), ACT.Copy).then_inc(gate_copied, 1)
            copy_bank(attn[:, bass.ds(tt * 2 + t2, 1), 0:TP].rearrange("p o c -> p (o c)"), P, 512).then_inc(tb_free, 1)
            assert tb[0] == TB_PER_T, tb

        @block.scalar
        def _(act):
            def cast(a, b, it):
                act.wait_ge(raw_full[a % 2], at_(16 * (a // 2 + 1), 8 * b, it))
                act.wait_ge(unit_done, at_(a + 1, b, it))
                act.activation(w_high[a % 2][:, :, :], w_raw[a % 2][:, :, :], ACT.Copy).then_inc(cast_done, 1)

            def done(a, b, it):
                act.wait_ge(unit_done, at_(a + 1 + 2, b, it))

            act.wait_ge(x_in, 32)
            act.wait_ge(consts, 1)
            act.wait_ge(dve_c, 1)
            for i in range(5):
                n = P if i < NB else TS
                if i:
                    act.wait_ge(x_sq, i)
                act.activation(junk[0:n, :], x_tok[0:n, i, :], ACT.Square, accum_out=x_ss[0:n, i:i + 1]).then_inc(x_sq, 1)
            act.wait_ge(x_var, 1)
            act.activation(x_rstd[:, :], x_rstd[:, :], ACT.Sqrt).then_inc(x_sd, 1)
            cast(0, 0, 0)
            cast(1, 0, 0)
            act.wait_ge(chan_tr, 1)
            act.activation(chan[:, :, :], ps[:, 3, 0:KT * NCV], ACT.Copy).then_inc(chan_done, 1)
            for i in range(5):
                n = P if i < NB else TS
                act.wait_ge(x_tr, i + 1)
                act.activation(x_high[:, :, i * P:i * P + n],
                               ps[:, 2 * (i % 2):2 * (i % 2) + 2, :].rearrange("p h (k c) -> p (h k) c", k=4)[:, :, 0:n],
                               ACT.Copy).then_inc(x_high_done, 1)
            act.wait_ge(state_tr, 1)
            act.activation(state[:, :, :, :].rearrange("p (h k) b r -> p h (k b r)", h=4), ps[:, 4:8, 0:480], ACT.Copy).then_inc(state_done, 1)

            with act.Fori(0, 4) as it:
                for j in range(4):
                    cast(U_GLU + j + 2, 4, it)
                    if j % 2:
                        done(U_GLU + j, 4, it)
                        act.wait_ge(u_done, at_(j // 2 + 1, 2, it))
                        act.activation(halves(glu_sig[:, j // 2, :]), pair(j), ACT.Sigmoid).then_inc(glu_sig_done, 1)

            with act.Fori(0, 2) as tt:
                for t2 in range(2):
                    act_pair(act, cast, done, tt, t2)

            def ln_square(k):
                act.wait_ge(centred, k + 1)
                if k >= 2:
                    act.wait_ge(csq_sum, k - 1)
                act.activation(ln_sq[:, k % 2, :], conv[:, k, :], ACT.Square).then_inc(csq_done, 1)

            for j in range(8):
                cast(U_CGATE + j + 2, 0, 0)
                if j == 3:
                    act.wait_ge(ut_done, 1)
                    act.activation(state_out[:, :].rearrange("r (h c) -> r h c", h=2), ps[0:CW - 1 + TS, 6:8, :], ACT.Copy).then_inc(ut_copied, 1)
                if j == 4:
                    act.wait_ge(var_done, 1)
                    act.activation(halves(ln_rstd[:, :]), ps[:, 6:8, 0:HT], ACT.Ln, bias=eps_col[:, :]).then_inc(ln_sd, 1)
                    act.wait_ge(ln_sd, 1)
                    act.activation(ln_rstd[:, :], ln_rstd[:, :], ACT.Exp, scale=-0.5).then_inc(ln_rs, 1)
                if j in (5, 6):
                    for k in range(4 * (j - 5), 4 * (j - 4)):
                        ln_silu(act, k)
                done(U_CGATE + j, 0, 0)
                act.activation(halves(gate_c[:, j, :]), pair(j % 2), ACT.Sigmoid).then_inc(tile_free, 1)
                if j in (1, 2):
                    for k in range(4 * (j - 1), 4 * j):
                        ln_square(k)
            for j in range(8):
                cast(U_COUT + j + 2, 0, 0)
                if j == 1:
                    act.wait_ge(c_low_done, KT)
                    act.activation(o_high[:, :, 0:TP], attn[:, :, 0:TP], ACT.Copy).then_inc(o_high_done, 1)
                if j == 5:
                    act.wait_ge(s_mx, 2)
                    act.activation(s_prob[:, :], ps[0:64, 4, 0:SKEYS], ACT.Exp, bias=s_small[0:64, 5:6],
                                   accum_out=s_small[0:64, 6:7]).then_inc(s_exp, 1)
                if j == 6:
                    act.wait_ge(s_ptr, 1)
                    act.activation(s_prob_t[:, 0:2, :], ps[:, 5, 0:128].rearrange("p (g c) -> p g c", g=2), ACT.Copy).then_inc(s_ptc, 1)
                    act.activation(s_prob_t[0:SROWS[2], 2, :], ps[0:SROWS[2], 5, 128:192], ACT.Copy).then_inc(s_ptc, 1)
            act.wait_ge(s_pv, 3)
            for hh in range(2):
                hp = slice(hh * E, (hh + 1) * E)
                act.activation(attn[hp, :, TP:T], ps[hp, 6, 0:64].rearrange("p (t b h) -> p t b h", t=4, h=2)[:, :, :, hh],
                               ACT.Copy).then_inc(s_out, 1)
            act.wait_ge(s_out, 2)
            act.activation(o_high[:, :, TP:T], attn[:, :, TP:T], ACT.Copy).then_inc(o_high_done, 1)
            act.wait_ge(gates_in, 16)
            for k in range(0, KT, 2):
                act.activation(gate_a[:, k:k + 2, :], gate_a[:, k:k + 2, :], ACT.Sigmoid).then_inc(agate_done, 2)
            with act.Fori(0, 2) as it:
                for j in range(2):
                    cast(U_AOUT + j + 2, 2, it)
                    for c in range(2):
                        n = 2 * j + c
                        act.wait_ge(merged, at_(n + 1, 4, it))
                        act.activation(c_high[:, bass.ds(it * 4 + n, 1), :], gate_a[:, bass.ds(it * 4 + n, 1), :], ACT.Copy).then_inc(m_high, 1)
            for k in range(KT):
                act.wait_ge(xt_full, k + 1)
                act.activation(x_feat[:, k, 0:TP], ps[:, 4 + k % 3, :], ACT.Copy).then_inc(xt_copied, 1)
            act.wait_ge(xt_full, KT + 1)
            act.activation(x_feat[:, :, TP:T], ps[:, 7, 0:KT * TS].rearrange("p (k c) -> p k c", k=KT), ACT.Copy).then_inc(xt_copied, 1)
            with act.Fori(0, 2) as it:
                for j in range(4):
                    cast(U_WO + j + 2, 4, it)
                    act.wait_ge(tile_free, at_(24 + j + 1 + 2, 4, it))
                    act.wait_ge(hss_sum, at_(j + 1, 4, it))
                    act.activation(h_sq[:, j % 2, :], h_feat[:, bass.ds(it * 4 + j, 1), :].rearrange("p o c -> p (o c)"), ACT.Square).then_inc(hsq_done, 1)
                    act.activation(x_high[:, bass.ds(it * 4 + j, 1), :], h_feat[:, bass.ds(it * 4 + j, 1), :], ACT.Copy,
                                   scale=chan[:, bass.ds(it * 4 + j, 1), C_N2:C_N2 + 1].rearrange("p o c -> p (o c)")).then_inc(hn_high, 1)
            for c in range(2):
                base = U_FF + 32 * c
                act.wait_ge(tile_free, 32 + 24 * c + 2)
                with act.Fori(0, 4) as it:
                    for j in range(4):
                        cast(base + j + 2, 4, it)
                        done(base + j, 4, it)
                        act.wait_ge(hid_done, at_(16 * c + j + 1, 4, it))
                        act.activation(halves(relu[:, j % 2, :]), pair(j % 2), ACT.Relu).then_inc(tile_free, 1)
                        act.wait_ge(tile_free, at_(32 + 24 * c + j + 1 + 2, 4, it))
                        act.activation(relu[:, j % 2, :], relu[:, j % 2, :], ACT.Square).then_inc(rsq_done, 1)
                        act.wait_ge(hid_done, at_(16 * c + j + 1 + 2, 4, it))
                        act.activation(hid_high[:, bass.ds(it * 4 + j, 1), :], hid[:, j % 2, :].rearrange("p (o c) -> p o c", o=1), ACT.Copy).then_inc(hid_hi, 1)
                if c == 0:
                    with act.Fori(0, 4) as it:
                        for j in range(4):
                            cast(base + 16 + j + 2, 4, it)
                else:
                    def y_copy(n):
                        act.wait_ge(y_tr, n + 1)
                        if n >= 2:
                            act.wait_ge(y_out[n % 2], 32 * (n // 2))
                        act.activation(y_tok[:, n % 2, :, :].rearrange("p b c -> p (b c)"), ps[:, 4 + n % 2, :], ACT.Copy).then_inc(y_half, 1)
                        act.activation(ys_tok[:, n % 2, :], ps[0:TS, 6 + n % 2, 0:P], ACT.Copy).then_inc(y_copied, 1)

                    for u in range(16):
                        if u < 14:
                            cast(base + 16 + u + 2, 0, 0)
                        if u % 2 and u >= 3:
                            y_copy(u // 2 - 1)
                    y_copy(7)

        def x_part(dve, i):
            n = P if i < NB else TS
            dve.wait_ge(x_high_done, i + 1)
            dve.tensor_tensor(x_low[:, :, i * P:i * P + n],
                              ps[:, 2 * (i % 2):2 * (i % 2) + 2, :].rearrange("p h (k c) -> p (h k) c", k=4)[:, :, 0:n],
                              x_high[:, :, i * P:i * P + n].bitcast(F32), ALU.subtract).then_inc(x_low_done, 1)

        def tap(dve, n, k, before):
            dst = conv[:, bass.ds(n, 1), 0:TP].rearrange("p o c -> p (o c)")
            src = u_in[:, bass.ds(n, 1), k:k + TP].rearrange("p o c -> p (o c)")
            w = chan[:, bass.ds(n, 1), k:k + 1].rearrange("p o c -> p (o c)")
            if k == 0:
                dve.tensor_scalar(dst, src, w, chan[:, bass.ds(n, 1), C_BIAS:C_BIAS + 1].rearrange("p o c -> p (o c)"),
                                  ALU.mult, ALU.add).then_inc(tap_done, 1)
            else:
                dve.wait_ge(tap_done, before)
                dve.scalar_tensor_tensor(dst, src, w, dst, ALU.mult, ALU.add).then_inc(tap_done, 1)

        def c_part(dve, k):
            dve.wait_ge(c_high_done, k + 1)
            dve.tensor_tensor(c_low[:, k, :], conv[:, k, :], c_high[:, k, :].bitcast(F32), ALU.subtract).then_inc(c_low_done, 1)

        def sample_scores(dve, g):
            n = SROWS[g]
            dve.wait_ge(kq_done, g + 1)
            kb = (kbuf, kbuf2, kbuf)[g]
            dve.tensor_reduce(s_score[0:n, g, :], kb[0:n, :, :].rearrange("p b (h e) -> p (b h) e", e=E), AX.X, ALU.add).then_inc(s_red, 1)

        def dve_pair(dve, split, tt, t2):
            def cnt(per_t, n):
                return at_(per_t * t2 + n, 2 * per_t, tt)

            cuts = conv_schedule()
            per_t = sum(len(c) for c in cuts)
            made = [0]

            def taps(slot):
                for tile, k in cuts[slot]:
                    n = tt * 4 + 2 * t2 + tile
                    before = at_(8 * GLU_TAPS + per_t * t2 + made[0] - 1, 2 * per_t, tt)
                    tap(dve, n, k, before)
                    made[0] += 1

            def norm(i):
                dve.wait_ge(rs_done, cnt(6, i + 1))
                dve.scalar_tensor_tensor(halves(qk[:, i, :]), pair(i % 3), qk_gain[:, i:i + 1], halves(rstd[:, i % 2, :]),
                                         ALU.mult, ALU.mult).then_inc(norm_done, 1)

            for i in range(9):
                split(U_QKV + PER_T * t2 + i + 2, 2 * PER_T, tt)
                if 1 <= i <= 6:
                    norm(i - 1)
                taps(i)

            def maximum(j):
                b = j % 4
                dve.wait_ge(scores, cnt(8, j + 1))
                dve.memset(job_sum[:, j % 2, 0:3], 0.0)
                for g in range(G):
                    n = (min(b, 1) + 1 if g == 0 else b + 1) * P
                    dve.tensor_tensor_reduce(ps[:, g, 512 - n:512], ps[:, g, 512 - n:512], mask[:, g, 512 - n:512], 1.0,
                                             LOWEST, ALU.add, ALU.max, job_max[:, j % 2, g:g + 1]).then_inc(masked, 1)
                dve.wait_ge(masked, cnt(24, 3 * j + 3))
                dve.tensor_reduce(job_max[:, j % 2, 3:4], job_max[:, j % 2, 0:3], AX.X, ALU.max, negate=True).then_inc(max_done, 1)

            def finish(j):
                dve.wait_ge(exp_done, cnt(8, j + 1))
                dve.tensor_reduce(job_sum[:, j % 2, 3:4], job_sum[:, j % 2, 0:3], AX.X, ALU.add).then_inc(sum_done, 1)
                dve.wait_ge(sum_done, cnt(8, j + 1))
                dve.reciprocal(job_sum[:, j % 2, 3:4], job_sum[:, j % 2, 3:4]).then_inc(rsum_done, 1)
                dve.wait_ge(rsum_done, cnt(8, j + 1))
                dve.wait_ge(o_done, cnt(8, j + 1))
                dve.tensor_scalar(o_tok[:, j % 4, (j // 4) * E:(j // 4 + 1) * E], ps[:, 3, 0:E], job_sum[:, j % 2, 3:4],
                                  None, ALU.mult).then_inc(o_norm, 1)

            maximum(0)
            for j in range(8):
                if j + 1 < 8:
                    maximum(j + 1)
                taps(9 + j)
                finish(j)
                if j % 4 == 3:
                    split(U_QKV + PER_T * t2 + 9 + j // 4 + 2, 2 * PER_T, tt)


        @block.vector
        def _(dve):
            def split(a, b, it):
                dve.wait_ge(cast_done, at_(a + 1, b, it))
                dve.tensor_tensor(w_low[a % 2][:, :, :], w_raw[a % 2][:, :, :], w_high[a % 2][:, :, :].bitcast(F32),
                                  ALU.subtract).then_inc(split_done, 1)

            def done(a, b, it):
                dve.wait_ge(unit_done, at_(a + 1 + 2, b, it))

            for i, (s, n) in enumerate(((split_done, 2), (unit_done, 2), (tile_free, 2), (tb_free, 2),
                                        (o_norm, 2), (u_done, 2), (y_copied, 2), (rows_free, 1))):
                dve.memset(credit[:, i:i + 1], 0.0).then_inc(s, n)
            dve.memset(s_small[:, 3:4], 0.0).then_inc(gate_copied, 2)
            dve.memset(s_small[:, 0:1], 0.0).then_inc(hid_done, 2)
            dve.memset(s_small[:, 1:2], 0.0).then_inc(hss_sum, 2)
            dve.memset(x_ss[:, :], 1.0).then_inc(dve_c, 1)

            dve.wait_ge(x_sq, 5)
            dve.wait_ge(dve_c, 1)
            dve.tensor_scalar(x_rstd[:, :], x_ss[:, :], 1.0 / D, EPS, ALU.mult, ALU.add).then_inc(x_var, 1)
            dve.wait_ge(x_sd, 1)
            dve.reciprocal(x_ss[:, :], x_rstd[:, :]).then_inc(x_rs, 1)
            dve.wait_ge(x_rs, 1)
            dve.wait_ge(gain_in, 16)
            for i in range(5):
                n = P if i < NB else TS
                if i >= 2:
                    dve.wait_ge(x_tr, i - 1)
                dve.scalar_tensor_tensor(xn_tok[0:n, i % 2, :], x_tok[0:n, i, :], x_ss[0:n, i:i + 1], gain1[0:n, :],
                                         ALU.mult, ALU.mult).then_inc(x_scaled, 1)
                if i == 1:
                    split(0, 0, 0)
                    split(1, 0, 0)
                if i >= 1:
                    x_part(dve, i - 1)
            x_part(dve, 4)

            dve.wait_ge(qkg_in, 16 * 12)
            dve.tensor_scalar(qk_gain[:, 0:G], qk_gain[:, 0:G], E ** -0.5, None, ALU.mult).then_inc(mask_done, 1)

            dve.wait_ge(chan_done, 1)
            dve.wait_ge(pool_c, 11)

            def glu_taps(n, second, part, it):
                for k in range(part * GLU_TAPS // 2, (part + 1) * GLU_TAPS // 2):
                    tap(dve, n, k, at_(second * GLU_TAPS + k, 2 * GLU_TAPS, it))

            with dve.Fori(0, 4) as it:
                for j in range(4):
                    split(U_GLU + j + 2, 4, it)
                    n = it * 2 + j // 2
                    if j % 2:
                        dve.wait_ge(glu_sig_done, at_(j // 2 + 1, 2, it))
                        dve.tensor_tensor(halves(u_in[:, bass.ds(n, 1), CW - 1:UW].rearrange("p o c -> p (o c)")), pair(j - 1),
                                          halves(glu_sig[:, j // 2, :]), ALU.mult).then_inc(u_done, 1)
                        dve.wait_ge(u_done, at_(j // 2 + 1 + 2, 2, it))
                        glu_taps(n, j // 2, 0, it)
                        if j == 3:
                            glu_taps(n, 1, 1, it)
                    elif j == 2:
                        glu_taps(it * 2, 0, 1, it)

            dve.wait_ge(state_done, 1)
            sc = conv[:, :, TP:T]
            taps_b = bass.AP(chan, 0, [[KT * NCV, P], [NCV, KT], [0, TS], [1, CW - 1]])
            last_b = bass.AP(chan, CW - 1, [[KT * NCV, P], [NCV, KT], [0, TS]])
            bias_b = bass.AP(chan, C_BIAS, [[KT * NCV, P], [NCV, KT], [0, TS]])
            dve.tensor_tensor(state[:, :, :, :], state[:, :, :, :], taps_b, ALU.mult).then_inc(sconv, 1)
            dve.wait_ge(sconv, 1)
            dve.tensor_reduce(sc, state[:, :, :, :], AX.X, ALU.add).then_inc(sconv, 1)
            dve.tensor_tensor(glu_sig[:, 0, 0:64].rearrange("p (k b) -> p k b", k=KT), u_in[:, :, CW - 1 + TP:UW], last_b, ALU.mult).then_inc(sconv, 1)
            dve.wait_ge(sconv, 3)
            dve.tensor_tensor(sc, sc, glu_sig[:, 0, 0:64].rearrange("p (k b) -> p k b", k=KT), ALU.add).then_inc(sconv, 1)
            dve.wait_ge(sconv, 4)
            dve.tensor_tensor(sc, sc, bias_b, ALU.add).then_inc(sconv, 1)

            n = 1
            for g in (1, 2):
                dve.tensor_scalar(dist_mod[:, :], dist[:, :], DIL[g] - 1, None, ALU.bitwise_and).then_inc(mask_done, 1)
                dve.wait_ge(mask_done, n + 1)
                dve.tensor_scalar(mod_mask[:, :], dist_mod[:, :], 0.0, NEG, ALU.is_gt, ALU.mult).then_inc(mask_done, 1)
                dve.wait_ge(mask_done, n + 2)
                dve.tensor_copy(mask[:, g, 0:3 * P].rearrange("p (b c) -> p b c", b=3), bass.AP(mod_mask, 0, [[P, P], [0, 3], [1, P]])).then_inc(mask_done, 1)
                dve.tensor_tensor(mask[:, g, 3 * P:4 * P], mod_mask[:, :], mask[:, 0, 3 * P:4 * P], ALU.min).then_inc(mask_done, 1)
                n += 4
                dve.wait_ge(mask_done, n)

            with dve.Fori(0, 2) as tt:
                for t2 in range(2):
                    dve_pair(dve, split, tt, t2)

            for j in range(8):
                split(U_CGATE + j + 2, 0, 0)
                if j in (1, 2):
                    dve.wait_ge(mean_done, 1)
                    for k in range(4 * (j - 1), 4 * j):
                        dve.tensor_tensor(halves(conv[:, k, :]), halves(conv[:, k, :]), ps[:, 4:6, 0:HT], ALU.subtract).then_inc(centred, 1)
                if j == 3:
                    sample_scores(dve, 0)
                if j == 4:
                    dve.wait_ge(ln_rs, 1)
                if j in (4, 5):
                    for k in range(4 * (j - 4), 4 * (j - 3)):
                        dve.tensor_tensor(conv[:, k, :], conv[:, k, :], ln_rstd[:, :], ALU.mult).then_inc(ln_scaled, 1)
                if j == 6:
                    for k in range(KT):
                        c_part(dve, k)
            for j in range(8):
                if j == 0:
                    dve.wait_ge(tile_free, 8 + 2)
                split(U_COUT + j + 2, 0, 0)
                done(U_COUT + j, 0, 0)
                gc = halves(gate_c[:, j, :])
                dve.tensor_tensor(gc, pair(j % 2), gc, ALU.mult).then_inc(tile_free, 1)
                if j in (0, 3):
                    sample_scores(dve, 1 + j // 3)
                if j == 2:
                    dve.wait_ge(o_high_done, 1)
                    dve.tensor_tensor(o_low[:, :, 0:TP], attn[:, :, 0:TP], o_high[:, :, 0:TP].bitcast(F32), ALU.subtract).then_inc(o_low_done, 1)
                if j == 5:
                    dve.wait_ge(s_tr, 1)
                    dve.reduce_max(s_small[0:64, 4:5], ps[0:64, 4, 0:SKEYS], AX.X).then_inc(s_mx, 1)
                    dve.wait_ge(s_mx, 1)
                    dve.tensor_scalar(s_small[0:64, 5:6], s_small[0:64, 4:5], -1.0, None, ALU.mult).then_inc(s_mx, 1)
                    dve.wait_ge(s_exp, 1)
                    dve.reciprocal(s_small[0:64, 7:8], s_small[0:64, 6:7]).then_inc(s_rs, 1)
                    dve.wait_ge(s_rs, 1)
                    dve.tensor_scalar(s_prob[:, :], s_prob[:, :], s_small[0:64, 7:8], None, ALU.mult).then_inc(s_pn, 1)
            dve.wait_ge(o_high_done, 2)
            dve.tensor_tensor(o_low[:, :, TP:T], attn[:, :, TP:T], o_high[:, :, TP:T].bitcast(F32), ALU.subtract).then_inc(o_low_done, 1)
            dve.wait_ge(agate_done, KT)
            with dve.Fori(0, 2) as it:
                for j in range(2):
                    split(U_AOUT + j + 2, 2, it)
                    done(U_AOUT + j, 2, it)
                    for c in range(2):
                        n = 2 * j + c
                        ga3 = gate_a[:, bass.ds(it * 4 + n, 1), :]
                        ga = halves(ga3.rearrange("p o c -> p (o c)"))
                        dve.tensor_tensor(ga, pair(c), ga, ALU.mult).then_inc(tile_free, 1)
                        dve.wait_ge(tile_free, at_(16 + n + 1 + 2, 4, it))
                        dve.tensor_tensor(ga3, ga3, gate_c[:, bass.ds(it * 4 + n, 1), :], ALU.add).then_inc(merged, 1)
                    for c in range(2):
                        n = 2 * j + c
                        dve.wait_ge(m_high, at_(n + 1, 4, it))
                        dve.tensor_tensor(c_low[:, bass.ds(it * 4 + n, 1), :], gate_a[:, bass.ds(it * 4 + n, 1), :],
                                          c_high[:, bass.ds(it * 4 + n, 1), :].bitcast(F32), ALU.subtract).then_inc(m_low, 1)
            with dve.Fori(0, 2) as it:
                for j in range(4):
                    split(U_WO + j + 2, 4, it)
                    done(U_WO + j, 4, it)
                    dve.wait_ge(xt_copied, KT + 1)
                    n = bass.ds(it * 4 + j, 1)
                    dve.tensor_tensor(halves(h_feat[:, n, :].rearrange("p o c -> p (o c)")), pair(j % 2),
                                      halves(x_feat[:, n, :].rearrange("p o c -> p (o c)")), ALU.add).then_inc(tile_free, 1)
                    dve.wait_ge(tile_free, at_(24 + j + 1 + 2, 4, it))
                    dve.wait_ge(hn_high, at_(j + 1, 4, it))
                    dve.scalar_tensor_tensor(x_low[:, n, :].rearrange("p o c -> p (o c)"), h_feat[:, n, :].rearrange("p o c -> p (o c)"),
                                             chan[:, n, C_N2:C_N2 + 1].rearrange("p o c -> p (o c)"),
                                             x_high[:, n, :].bitcast(F32).rearrange("p o c -> p (o c)"), ALU.mult, ALU.subtract).then_inc(hn_low, 1)
            for c in range(2):
                base = U_FF + 32 * c

                def ff1(b, it):
                    for j in range(4):
                        split(base + j + 2, b, it)
                        if c == 0 and b == 0 and j == 0:
                            dve.wait_ge(hss_done, 1)
                            dve.tensor_scalar(halves(h_rs2[:, :]), ps[:, 4:6, 0:HT], EPS, None, ALU.add).then_inc(h_rs, 1)
                            dve.wait_ge(h_rs, 1)
                            dve.reciprocal(h_rs2[:, :], h_rs2[:, :]).then_inc(h_rs, 1)
                            dve.wait_ge(h_rs, 2)
                        dve.wait_ge(rsq_done, at_(16 * c + j + 1, b, it))
                        dve.tensor_tensor(hid[:, j % 2, :], relu[:, j % 2, :], h_rs2[:, :], ALU.mult).then_inc(hid_done, 1)
                        dve.wait_ge(hid_hi, at_(16 * c + j + 1, b, it))
                        n = bass.ds(it * b + j, 1)
                        dve.tensor_tensor(hid_low[:, n, :].rearrange("p o c -> p (o c)"), hid[:, j % 2, :],
                                          hid_high[:, n, :].bitcast(F32).rearrange("p o c -> p (o c)"), ALU.subtract).then_inc(hid_lo, 1)

                if c == 0:
                    ff1(0, 0)
                with dve.Fori(1 - c, 4) as it:
                    ff1(4, it)
                dve.wait_ge(tile_free, 48 + 24 * c + 2)
                if c == 0:
                    with dve.Fori(0, 4) as it:
                        for j in range(4):
                            split(base + 16 + j + 2, 4, it)
                            if j % 2:
                                done(base + 16 + j, 4, it)
                                hf = halves(h_feat[:, bass.ds(it * 2 + j // 2, 1), :].rearrange("p o c -> p (o c)"))
                                dve.tensor_tensor(hf, pair(j // 2), hf, ALU.add).then_inc(tile_free, 1)
                else:
                    for n in range(8):
                        for j in (2 * n, 2 * n + 1):
                            if j < 14:
                                split(base + 16 + j + 2, 0, 0)
                        done(base + 16 + 2 * n + 1, 0, 0)
                        if n >= 2:
                            dve.wait_ge(y_tr, n - 1)
                        dve.tensor_tensor(halves(y_feat[:, n % 2, :]), pair(n % 2), halves(h_feat[:, n, :]), ALU.add).then_inc(tile_free, 1)

        @block.gpsimd
        def _(pool):
            made = [0]

            def link(ins):
                made[0] += 1
                ins.then_inc(pool_c, 1)
                pool.wait_ge(pool_c, made[0])

            link(pool.memset(ident[:, :], 0.0))
            pool.affine_select(out=ident[:, :], in_=ident[:, :], compare_op=ALU.not_equal, fill=1.0, base=0,
                               pattern=[[-1, P]], channel_multiplier=1).then_inc(pool_c, 1)
            made[0] += 1
            pool.memset(eps_col[:, :], EPS).then_inc(pool_c, 1)
            made[0] += 1
            pool.wait_ge(pool_c, made[0])
            pool.memset(ones[:, :], 1.0 / D).then_inc(consts, 1)
            link(pool.memset(head_ones[:, :], 0.0))
            link(pool.memset(head_ones[0:E, 0:E], 1.0))
            link(pool.memset(head_ones[E:P, E:P], 1.0))
            link(pool.memset(mask[:, 0, :], 0.0))
            pool.memset(u_in[:, :, 0:CW - 1], 0.0).then_inc(pool_c, 1)
            pool.affine_select(out=mask[:, 0, 2 * P:3 * P], in_=mask[:, 0, 2 * P:3 * P], compare_op=ALU.is_ge, fill=NEG, base=0,
                               pattern=[[1, P]], channel_multiplier=-1).then_inc(pool_c, 1)
            made[0] += 2
            pool.affine_select(out=mask[:, 0, 3 * P:4 * P], in_=mask[:, 0, 3 * P:4 * P], compare_op=ALU.is_ge, fill=NEG, base=0,
                               pattern=[[-1, P]], channel_multiplier=1).then_inc(pool_c, 1)
            pool.iota(dist[:, :], pattern=[[-1, P]], base=P, channel_multiplier=1).then_inc(pool_c, 1)
            for half in range(2):
                hp = slice(half * E, (half + 1) * E)
                for g in range(G):
                    pool.dma_start(qk_gain[hp, g:g + 1], q_norm_g[0, g].rearrange("(e o) -> e o", o=1)).then_inc(qkg_in, 16)
                    pool.dma_start(qk_gain[hp, G + g:G + g + 1], k_norm_g[0, g].rearrange("(e o) -> e o", o=1)).then_inc(qkg_in, 16)

            with pool.Fori(0, 4) as t:
                col = bass.ds(t * P, P)
                pool.wait_ge(tb_free, t * TB_PER_T + 21 + 2)
                for src, dst in ((k_tok, pk), (v_tok, pv)):
                    pool.dma_start(rows(dst[0])[0][:, col], src[:, NB - 1, 0, :]).then_inc(kv_stored, 16)
                    for g in (1, 2):
                        pool.dma_start(rows(dst[g])[0].rearrange("(b p) c -> p b c", p=P)[:, :, col], src[:, :, g, :]).then_inc(kv_stored, 16)
                for n in range(3):
                    pool.dma_start(scratch[n][:, :, col], new_tok[:, n, :, :]).then_inc(new_stored, 16)
                pool.wait_ge(gate_copied, 2 * t + 4)
                pool.dma_start(gate_rows[:, bass.ds(t * 2, 2), :], gate_stage[:, :, :]).then_inc(gates_stored, 16)
                pool.wait_ge(gates_stored, 16 * t + 16)
                pool.wait_ge(kv_stored, 96 * t + 96)
                pool.wait_ge(new_stored, 48 * t + 48)
                pool.tensor_tensor(pool_mark[:, :], eps_col[:, :], eps_col[:, :], ALU.mult).then_inc(rows_free, 1)

            pool.wait_ge(tap_done, 8 * CW)
            pool.wait_ge(sconv, 5)
            pool.tensor_tensor(c_sum[:, :], conv[:, 0, :], conv[:, 1, :], ALU.add).then_inc(c_summed, 2)
            for k in range(2, KT):
                pool.wait_ge(c_summed, k)
                pool.tensor_tensor(c_sum[:, :], c_sum[:, :], conv[:, k, :], ALU.add).then_inc(c_summed, 1)

            pool.wait_ge(new_stored, 16 * 3 * 4)
            qrow, krow, vrow = scratch[0], scratch[1], scratch[2]

            def cache_tile(src, g):
                a = rows(src[g])
                if g == 0:
                    return a.rearrange("b r c -> r b c")
                d = DIL[g]
                return a.rearrange("b (r d) c -> r d b c", d=d)[:, 0, :, :]

            def load_keys(g):
                n = (128, 128, 64)[g]
                kb = (kbuf, kbuf2, kbuf)[g]
                pool.dma_start(kb[0:n, :, :], cache_tile(cache_k, g)).then_inc(k_in, 16)
                pool.dma_start(qbuf[0:n, :, :], bass.AP(qrow.tensor, qrow.offset + g * AW, [[0, n], [G * AW, TS], [1, AW]])).then_inc(q_in, 16)
                if g == 2:
                    pool.dma_start(kb[64:67, :, :], krow.rearrange("b g c -> g b c")).then_inc(kn_in, 16)
                    pool.dma_start(qbuf[64:67, :, :], qrow.rearrange("b g c -> g b c")).then_inc(qn_in, 16)

            def products(g):
                n = SROWS[g]
                kb = (kbuf, kbuf2, kbuf)[g]
                pool.wait_ge(k_in, 16 * (g + 1))
                pool.wait_ge(q_in, 16 * (g + 1))
                if g == 2:
                    pool.wait_ge(kn_in, 16)
                    pool.wait_ge(qn_in, 16)
                pool.tensor_tensor(kb[0:n, :, :], kb[0:n, :, :], qbuf[0:n, :, :], ALU.mult).then_inc(kq_done, 1)

            pool.wait_ge(unit_done, 2 + U_CGATE + 1)
            pool.wait_ge(kv_stored, 16 * 6 * 4)
            load_keys(0)
            for k in range(KT):
                pool.wait_ge(csq_done, k + 1)
                if k == 0:
                    pool.tensor_copy(ln_sum[:, :], ln_sq[:, 0, :]).then_inc(csq_sum, 1)
                else:
                    pool.wait_ge(csq_sum, k)
                    pool.tensor_tensor(ln_sum[:, :], ln_sum[:, :], ln_sq[:, k % 2, :], ALU.add).then_inc(csq_sum, 1)
            products(0)
            pool.wait_ge(kq_done, 1)
            load_keys(1)
            pool.wait_ge(ut_copied, 1)
            pool.dma_start(p_conv[0, 0], state_out[0:CW - 1, :]).then_inc(conv_out, 16)
            pool.dma_start(s_conv[0][:, CW - 2, :], state_out[CW - 1:CW - 1 + TS, :]).then_inc(conv_out, 16)
            pool.dma_start(s_conv[0][:, 0:CW - 2, :], state_conv[0][:, 1:CW - 1, :]).then_inc(new_rows, 16)
            for g in range(G):
                at_row = CACHE[g] - 1 if g < 2 else CACHE[g]
                pool.dma_start(rows(sk[g])[:, at_row, :], krow[:, g, :]).then_inc(new_rows, 16)
                pool.dma_start(rows(sv[g])[:, at_row, :], vrow[:, g, :]).then_inc(new_rows, 16)
            products(1)
            pool.wait_ge(kq_done, 2)
            pool.wait_ge(s_red, 1)
            load_keys(2)
            pool.wait_ge(s_red, 2)
            pool.dma_start(kbuf2[:, :, :], cache_tile(cache_v, 0)).then_inc(v_in[0], 16)
            products(2)
            pool.wait_ge(kq_done, 3)
            pool.dma_start(qbuf[:, :, :], cache_tile(cache_v, 1)).then_inc(v_in[1], 16)
            pool.wait_ge(s_red, 3)
            pool.dma_start(kbuf[0:64, :, :], cache_tile(cache_v, 2)).then_inc(v_in[2], 16)
            pool.dma_start(kbuf[64:67, :, :], vrow.rearrange("b g c -> g b c")).then_inc(vn_in, 16)
            pool.wait_ge(s_pv, 1)
            pool.dma_start(gate_a[:, :, :], gate_rows).then_inc(gates_in, 16)
            pool.wait_ge(s_pv, 3)
            pool.dma_start(x_tok2[:, 0:NB, :], x_prompt[0].rearrange("(b p) d -> p b d", p=P)).then_inc(x2_in, 16)
            pool.dma_start(x_tok2[0:TS, NB, :], x_sample.rearrange("b s d -> (b s) d")).then_inc(x2_in, 16)
            for k in range(KT):
                pool.wait_ge(hsq_done, k + 1)
                if k == 0:
                    pool.tensor_copy(h_ss[:, :], h_sq[:, 0, :]).then_inc(hss_sum, 1)
                else:
                    pool.wait_ge(hss_sum, k + 2)
                    pool.tensor_tensor(h_ss[:, :], h_ss[:, :], h_sq[:, k % 2, :], ALU.add).then_inc(hss_sum, 1)
            yp = y_prompt[0].rearrange("(b p) d -> p b d", p=P)
            ys = y_sample.rearrange("b s d -> (b s) d")
            for n in range(8):
                pool.wait_ge(y_half, n + 1)
                pool.wait_ge(y_copied, n + 1 + 2)
                pool.dma_start(yp[:, :, n * P:(n + 1) * P], y_tok[:, n % 2, :, :]).then_inc(y_out[n % 2], 16)
                pool.dma_start(ys[:, n * P:(n + 1) * P], ys_tok[:, n % 2, :]).then_inc(y_out[n % 2], 16)


def at_(a, b=0, it=0):
    return a + b * it if b else a


_INS = ['x_prompt', 'x_sample', 'cache_k1', 'cache_v1', 'cache_k2', 'cache_v2', 'cache_k3', 'cache_v3', 'state_conv',
        'norm1_g', 'w_in', 'q_norm_g', 'k_norm_g', 'conv_w', 'conv_b', 'conv_ln_g', 'conv_ln_b', 'w_attn_out',
        'w_conv_out', 'w_o', 'norm2_g', 'w_ff1', 'w_ff2']
_OUTS = [(1, TP, D), (TS, 1, D),
         (1, 1, 128, HEADS, E), (1, 1, 128, HEADS, E), (1, 1, TP, HEADS, E), (1, 1, TP, HEADS, E),
         (1, 1, TP, HEADS, E), (1, 1, TP, HEADS, E), (1, 1, CW - 1, D),
         (1, TS, 128, HEADS, E), (1, TS, 128, HEADS, E), (1, TS, 512, HEADS, E), (1, TS, 512, HEADS, E),
         (1, TS, 1025, HEADS, E), (1, TS, 1025, HEADS, E), (1, TS, CW - 1, D)]


def kernel(**inputs):
    import numpy as _np
    import concourse.bacc as _bacc
    from concourse import mybir as _mybir
    from concourse.bass_utils import run_bass_kernel_spmd as _run

    nc = _bacc.Bacc("TRN2", target_bir_lowering=False, num_devices=1)
    arrays, args = {}, []
    for name in _INS:
        a = _np.ascontiguousarray(inputs[name])
        arrays[f"in_{name}_dram"] = a
        args.append(nc.dram_tensor(f"in_{name}_dram", a.shape, _mybir.dt.from_np(a.dtype), kind="ExternalInput").ap())
    for i, shape in enumerate(_OUTS):
        args.append(nc.dram_tensor(f"out_{i}_dram", shape, _mybir.dt.float32, kind="ExternalOutput").ap())
    build_step(nc, *args)
    r = _run(nc, [arrays], core_ids=[0])
    return tuple(r.results[0][f"out_{i}_dram"] for i in range(len(_OUTS)))
```

```python
from contextlib import ExitStack

import concourse.bass as bass
from concourse import mybir

F32 = mybir.dt.float32
F32R = mybir.dt.float32r
I32 = mybir.dt.int32
ALU = mybir.AluOpType
ACT = mybir.ActivationFunctionType
AX = mybir.AxisListType

P = 128
D = 1024
KT = D // P
TP = 512
NB = TP // P
TS = 8
T = TP + TS
HT = T // 2
G = 3
HEADS = 8
E = 64
AW = HEADS * E
CW = 31
DFF = 4096
EPS = 1e-6
NEG = -1e30
LOWEST = -3e38
DIL = (1, 4, 16)
CACHE = (128, 512, 1024)
SROWS = (128, 128, 67)
SKEYS = sum(SROWS)

COL_Q, COL_K, COL_V = 0, G * AW, 2 * G * AW
COL_GA = 3 * G * AW
COL_GB = COL_GA + D
COL_GATE_A = COL_GB + D
COL_GATE_C = COL_GATE_A + D

U_GLU = 0
U_QKV = U_GLU + 16
PER_T = 9 + 2
U_CGATE = U_QKV + 4 * PER_T
U_COUT = U_CGATE + 8
U_AOUT = U_COUT + 8
U_WO = U_AOUT + 4
U_FF = U_WO + 8
UNITS = U_FF + 64

GLU_TAPS = 8
SLOT_TAPS = 3
GATE_PARTS = ((1, 1), (1, 1), (1, 0), (1, 0), (1, 1), (1, 0), (1, 0), (1, 1))
GATE_JOB = (1, 7)
TB_PER_T = 38


def conv_schedule():
    taps = [(tile, tap) for tap in range(GLU_TAPS, CW) for tile in range(2)]
    cuts, at = [], 0
    for slot in range(17):
        n = 2 if slot == 0 else 3
        cuts.append(taps[at:at + n])
        at += n
    assert at >= len(taps)
    return cuts


def build_step(nc, x_prompt, x_sample, cache_k1, cache_v1, cache_k2, cache_v2, cache_k3, cache_v3,
               state_conv, norm1_g, w_in, q_norm_g, k_norm_g, conv_w, conv_b, conv_ln_g, conv_ln_b,
               w_attn_out, w_conv_out, w_o, norm2_g, w_ff1, w_ff2,
               y_prompt, y_sample, pk1, pv1, pk2, pv2, pk3, pv3, p_conv,
               sk1, sv1, sk2, sv2, sk3, sv3, s_conv):
    cache_k, cache_v = (cache_k1, cache_k2, cache_k3), (cache_v1, cache_v2, cache_v3)
    pk, pv = (pk1, pk2, pk3), (pv1, pv2, pv3)
    sk, sv = (sk1, sk2, sk3), (sv1, sv2, sv3)

    def rows(a):
        return a[0].rearrange("b r h e -> b r (h e)")

    ctx = ExitStack()
    with ctx:
        def sem(name):
            return ctx.enter_context(nc.semaphore(name))

        BASE = 16512

        def place(name, shape, dt, at):
            size = 4
            for n in shape[1:]:
                size *= n
            at = (at + 31) // 32 * 32
            return nc.alloc_sbuf_tensor_at(name, shape, dt, offset=BASE + at), at + size

        pos = 0
        x_high, pos = place("x_high", [P, KT, T], F32R, pos)
        x_low, pos = place("x_low", [P, KT, T], F32R, pos)
        w_raw0, pos = place("w_raw0", [P, KT, P], F32, pos)
        w_raw1, pos = place("w_raw1", [P, KT, P], F32, pos)
        w_high0, pos = place("w_high0", [P, KT, P], F32R, pos)
        w_high1, pos = place("w_high1", [P, KT, P], F32R, pos)
        w_low0, pos = place("w_low0", [P, KT, P], F32R, pos)
        w_low1, pos = place("w_low1", [P, KT, P], F32R, pos)
        w_raw, w_high, w_low = (w_raw0, w_raw1), (w_high0, w_high1), (w_low0, w_low1)
        ident, pos = place("ident", [P, P], F32, pos)
        ones, pos = place("ones", [P, P], F32, pos)
        head_ones, pos = place("head_ones", [P, P], F32, pos)
        mask, pos = place("mask", [P, G, TP], F32, pos)
        dist, pos = place("dist", [P, P], I32, pos)
        dist_mod, pos = place("dist_mod", [P, P], I32, pos)
        mod_mask, pos = place("mod_mask", [P, P], F32, pos)
        qk_gain, pos = place("qk_gain", [P, 6], F32, pos)
        NCV = CW + 4
        chan, pos = place("chan", [P, KT, NCV], F32, pos)
        C_BIAS, C_LNG, C_LNB, C_N2 = CW, CW + 1, CW + 2, CW + 3
        eps_col, pos = place("eps_col", [P, 1], F32, pos)
        credit, pos = place("credit", [P, 8], F32, pos)
        s_small, pos = place("s_small", [P, 16], F32, pos)
        pool_mark, pos = place("pool_mark", [P, 2], F32, pos)
        x_ss, pos = place("x_ss", [P, 5], F32, pos)
        x_rstd, pos = place("x_rstd", [P, 5], F32, pos)
        x_rinv, pos = place("x_rinv", [P, 5], F32, pos)
        job_max, pos = place("job_max", [P, 2, 4], F32, pos)
        job_sum, pos = place("job_sum", [P, 2, 4], F32, pos)
        pos = (pos + 31) // 32 * 32
        UW = CW - 1 + T
        U0 = pos
        u_in, pos = place("u_in", [P, KT, UW], F32, pos)
        conv, pos = place("conv", [P, KT, T], F32, pos)
        attn, pos = place("attn", [P, 4, T], F32, pos)
        QR = pos
        at = QR
        x_tok, at = place("x_tok", [P, 5, D], F32, at)
        gain1, at = place("gain1", [P, D], F32, at)
        junk, at = place("junk", [P, D], F32, at)
        xn_tok, at = place("xn_tok", [P, 2, D], F32, at)
        chan_rows, at = place("chan_rows", [NCV, D], F32, at)
        state_rows, at = place("state_rows", [120, 2, D], F32, at)
        at = QR
        qk, at = place("qk", [P, 6, T], F32, at)
        square, at = place("square", [P, 2, T], F32, at)
        rstd, at = place("rstd", [P, 2, T], F32, at)
        v_feat, at = place("v_feat", [P, G, T], F32, at)
        k_tok, at = place("k_tok", [P, NB, G, P], F32, at)
        v_tok, at = place("v_tok", [P, NB, G, P], F32, at)
        new_tok, at = place("new_tok", [TS, 3, G, P], F32, at)
        probs, at = place("probs", [P, 2, 1280], F32, at)
        probs_t, at = place("probs_t", [P, 2, 1280], F32, at)
        o_tok, at = place("o_tok", [P, NB, P], F32, at)
        glu_sig, at = place("glu_sig", [P, 2, T], F32, at)
        gate_stage = glu_sig
        GEND = at
        state, at = place("state", [P, KT, TS, CW - 1], F32, at)
        assert at <= 212863 - 64, at
        c_high, _ = place("c_high", [P, KT, T], F32R, U0)
        at = QR
        c_low, at = place("c_low", [P, KT, T], F32R, at)
        KB = at
        kbuf, at = place("kbuf", [P, TS, AW], F32, at)
        qbuf, at = place("qbuf", [P, TS, AW], F32, at)
        _, at2 = place("x_tok2_", [P, 5, D], F32, KB)
        x_tok2 = nc.alloc_sbuf_tensor_at("x_tok2", [P, 5, D], F32, offset=BASE + KB)
        x_feat, at2 = place("x_feat", [P, KT, T], F32, at2)
        at = max(at, at2)
        gate_c, at = place("gate_c", [P, KT, T], F32, at)
        h_feat = nc.alloc_sbuf_tensor_at("h_feat", [P, KT, T], F32, offset=BASE + at - 4 * KT * T)
        GA = at
        gate_a, at = place("gate_a", [P, KT, T], F32, at)
        s_score, at = place("s_score", [P, G, TS * HEADS], F32, at)
        s_prob, at = place("s_prob", [TS * HEADS, SKEYS], F32, at)
        s_prob_t, at = place("s_prob_t", [P, G, TS * HEADS], F32, at)
        SMALL = at
        assert at <= 212863 - 64, at
        kbuf2, at = place("kbuf2", [P, TS, AW], F32, GEND)
        assert at <= GA + 4 * KT * T
        at = QR
        ln_sq, at = place("ln_sq", [P, 4, T], F32, at)
        ln_sum, at = place("ln_sum", [P, T], F32, at)
        at = SMALL
        ln_rstd, at = place("ln_rstd", [P, T], F32, at)
        c_sum, at = place("c_sum", [P, 2, T], F32, at)
        state_out, at = place("state_out", [CW - 1 + TS, D], F32, at)
        assert at <= 212863 - 64, at
        o_high = nc.alloc_sbuf_tensor_at("o_high", [P, 4, T], F32R, offset=BASE + U0 + 4 * KT * UW)
        o_low = nc.alloc_sbuf_tensor_at("o_low", [P, 4, T], F32R, offset=BASE + U0 + 4 * KT * UW + 16 * T)
        at = GA
        h_sq, at = place("h_sq", [P, 2, T], F32, at)
        h_ss, at = place("h_ss", [P, T], F32, at)
        h_rs2, at = place("h_rs2", [P, T], F32, at)
        relu, at = place("relu", [P, 2, T], F32, at)
        hid, at = place("hid", [P, 2, T], F32, at)
        assert at <= 212863 - 64, at
        hid_high, at = place("hid_high", [P, 16, T], F32R, U0)
        hid_low, at = place("hid_low", [P, 16, T], F32R, at)
        assert at <= GA - 4 * KT * T, (at, GA)
        y_feat, at = place("y_feat", [P, 2, T], F32, GA + 4 * T * 8)
        y_tok, at = place("y_tok", [P, 2, NB, P], F32, at)
        ys_tok, at = place("ys_tok", [TS, 2, P], F32, at)
        assert at <= 212863 - 64, at

        ps = ctx.enter_context(nc.psum_tensor("ps", [P, 8, 512], F32))

        def pair(n):
            return ps[:, 2 * n:2 * n + 2, 0:HT]

        def halves(a):
            return a.rearrange("p (h c) -> p h c", h=2)

        gate_rows = nc.dram_tensor("gate_rows", [P, KT, T], F32).ap()
        scratch = nc.dram_tensor("new_qkv", [3, TS, G, AW], F32).ap()

        raw_full = [sem("raw_full0"), sem("raw_full1")]
        cast_done = sem("cast_done")
        split_done = sem("split_done")
        unit_done = sem("unit_done")
        tile_free = sem("tile_free")
        x_in = [sem("x_in%d" % i) for i in range(5)]
        gain_in = sem("gain_in")
        chan_in = sem("chan_in")
        state_in = sem("state_in")
        qkg_in = sem("qkg_in")
        consts = sem("consts")
        pool_c = sem("pool_c")
        dve_c = sem("dve_c")
        mask_done = sem("mask_done")
        x_sq = sem("x_sq")
        x_var = sem("x_var")
        x_sd = sem("x_sd")
        x_rs = sem("x_rs")
        x_scaled = sem("x_scaled")
        x_tr = sem("x_tr")
        x_high_done = sem("x_high_done")
        x_low_done = sem("x_low_done")
        chan_tr = sem("chan_tr")
        chan_done = sem("chan_done")
        state_tr = sem("state_tr")
        state_done = sem("state_done")
        glu_sig_done = sem("glu_sig_done")
        u_done = sem("u_done")
        tap_done = sem("tap_done")
        sconv = sem("sconv")
        sq_done = sem("sq_done")
        tb_full = sem("tb_full")
        tb_free = sem("tb_free")
        rs_done = sem("rs_done")
        norm_done = sem("norm_done")
        v_done = sem("v_done")
        scores = sem("scores")
        masked = sem("masked")
        max_done = sem("max_done")
        exp_done = sem("exp_done")
        sum_done = sem("sum_done")
        rsum_done = sem("rsum_done")
        o_done = sem("o_done")
        o_norm = sem("o_norm")
        kv_stored = sem("kv_stored")
        new_stored = sem("new_stored")
        rows_free = sem("rows_free")
        c_summed = sem("c_summed")
        mean_done = sem("mean_done")
        centred = sem("centred")
        csq_done = sem("csq_done")
        csq_sum = sem("csq_sum")
        var_done = sem("var_done")
        ln_sd = sem("ln_sd")
        ln_rs = sem("ln_rs")
        ln_scaled = sem("ln_scaled")
        silu_done = sem("silu_done")
        c_high_done = sem("c_high_done")
        c_low_done = sem("c_low_done")
        ut_done = sem("ut_done")
        ut_copied = sem("ut_copied")
        gate_copied = sem("gate_copied")
        gates_stored = sem("gates_stored")
        gates_in = sem("gates_in")
        agate_done = sem("agate_done")
        abranch = sem("abranch")
        merged = sem("merged")
        m_high = sem("m_high")
        m_low = sem("m_low")
        o_high_done = sem("o_high_done")
        o_low_done = sem("o_low_done")
        k_in = sem("k_in")
        q_in = [sem("q_in0"), sem("q_in1")]
        kq_done = sem("kq_done")
        s_red = sem("s_red")
        s_tr = sem("s_tr")
        s_mx = sem("s_mx")
        s_exp = sem("s_exp")
        s_rs = sem("s_rs")
        s_pn = sem("s_pn")
        s_ptr = sem("s_ptr")
        s_ptc = sem("s_ptc")
        v_weighted = sem("v_weighted")
        v_sum = sem("v_sum")
        v_in = [sem("v_in0"), sem("v_in1"), sem("v_in2")]
        vn_in = sem("vn_in")
        s_pv = sem("s_pv")
        s_out = sem("s_out")
        x2_in = sem("x2_in")
        xt_full = sem("xt_full")
        xt_copied = sem("xt_copied")
        hsq_done = sem("hsq_done")
        hss_sum = sem("hss_sum")
        hss_done = sem("hss_done")
        h_rs = sem("h_rs")
        hn_high = sem("hn_high")
        hn_low = sem("hn_low")
        relu_done = sem("relu_done")
        rsq_done = sem("rsq_done")
        hid_done = sem("hid_done")
        hid_hi = sem("hid_hi")
        hid_lo = sem("hid_lo")
        y_tr = sem("y_tr")
        y_copied = sem("y_copied")
        y_half = sem("y_half")
        y_last = sem("y_last")
        y_out = [sem("y_out0"), sem("y_out1")]
        copies = sem("copies")
        conv_out = sem("conv_out")
        new_rows = sem("new_rows")

        win = w_in[0].rearrange("(k p) n -> p k n", p=P)
        wao = w_attn_out[0].rearrange("(k p) n -> p k n", p=P)
        wco = w_conv_out[0].rearrange("(k p) n -> p k n", p=P)
        wo = w_o[0].rearrange("(k p) n -> p k n", p=P)
        wf1 = w_ff1[0].rearrange("(k p) n -> p k n", p=P)
        wf2 = w_ff2[0].rearrange("(q k p) n -> q p k n", q=4, p=P)

        block = ctx.enter_context(nc.Block())

        @block.sync
        def _(sp):
            for b in range(NB):
                sp.dma_start(x_tok[:, b, :], x_prompt[0, b * P:(b + 1) * P, :]).then_inc(x_in[b], 16)
            sp.dma_start(x_tok[0:TS, NB, :], x_sample.rearrange("b s d -> (b s) d")).then_inc(x_in[NB], 16)
            sp.dma_start(gain1[:, :], norm1_g.to_broadcast([P, D])).then_inc(gain_in, 16)

            def load(a, b, it, src, dst=None):
                sp.wait_ge(split_done, at_(a + 1, b, it))
                sp.dma_start(w_raw[a % 2][:, :, :] if dst is None else dst, src).then_inc(raw_full[a % 2], 16)

            def copy_rows(g, which, b):
                src = rows((cache_k, cache_v)[which][g])
                dst = rows((sk, sv)[which][g])
                n = CACHE[g] - 1 if g < 2 else CACHE[g]
                skip = CACHE[g] - n
                sp.dma_start(dst[bass.ds(b, 1), 0:n, :], src[bass.ds(b, 1), skip:skip + n, :]).then_inc(copies, 16)

            for u in range(2):
                load(u, 0, 0, win[:, :, COL_GA + u * D:COL_GA + u * D + P])
            sp.dma_start(chan_rows[0:CW, :], conv_w[0]).then_inc(chan_in, 16)
            for r, vec in ((C_BIAS, conv_b), (C_LNG, conv_ln_g), (C_LNB, conv_ln_b), (C_N2, norm2_g)):
                sp.dma_start(chan_rows[r:r + 1, :], vec).then_inc(chan_in, 16)
            sp.dma_start(state_rows[:, :, :], state_conv[0].rearrange("(h b) r c -> (b r) h c", h=2)).then_inc(state_in, 16)
            for u in range(2, 4):
                load(u, 0, 0, win[:, :, COL_GA + (u % 2) * D + P:COL_GA + (u % 2) * D + 2 * P])
            with sp.Fori(1, 4) as it:
                for j in range(4):
                    load(U_GLU + j, 4, it, win[:, :, bass.ds(it * 2 * P + COL_GA + (j % 2) * D + (j // 2) * P, P)])
            with sp.Fori(0, 2) as tt:
                for t2 in range(2):
                    for i in range(9):
                        col = (i // G) * G * AW + (i % G) * AW + t2 * P
                        load(U_QKV + PER_T * t2 + i, 2 * PER_T, tt, win[:, :, bass.ds(tt * 2 * P + col, P)])
                        if i < 8:
                            copy_rows(i // 4, i // 2 % 2, tt * 4 + 2 * t2 + i % 2)
                        else:
                            copy_rows(2, 1, tt * 4 + 2 * t2)
                            copy_rows(2, 1, tt * 4 + 2 * t2 + 1)
                    for i in range(2):
                        load(U_QKV + PER_T * t2 + 9 + i, 2 * PER_T, tt,
                             win[:, :, bass.ds(tt * 4 * P + COL_GATE_A + (2 * t2 + i) * P, P)])
            with sp.Fori(0, 2) as it:
                for j in range(4):
                    load(U_CGATE + j, 4, it, win[:, :, bass.ds(it * 4 * P + COL_GATE_C + j * P, P)])
            with sp.Fori(0, 2) as it:
                for j in range(4):
                    load(U_COUT + j, 4, it, wco[:, :, bass.ds(it * 4 * P + j * P, P)])
            with sp.Fori(0, 2) as it:
                for j in range(2):
                    load(U_AOUT + j, 2, it, wao[:, :, bass.ds(it * 4 * P + j * 2 * P, 2 * P)],
                         w_raw[j][:, :, :].rearrange("p k n -> p (k n)").rearrange("p (k n) -> p k n", k=4))
            with sp.Fori(0, 2) as it:
                for j in range(4):
                    load(U_WO + j, 4, it, wo[:, :, bass.ds(it * 4 * P + j * P, P)])
            for c in range(2):
                with sp.Fori(0, 4) as it:
                    for j in range(4):
                        load(U_FF + 32 * c + j, 4, it, wf1[:, :, bass.ds(it * 4 * P + 16 * c * P + j * P, P)])
                    copy_rows(2, 0, it + 4 * c)
                with sp.Fori(0, 4) as it:
                    for j in range(4):
                        load(U_FF + 32 * c + 16 + j, 4, it,
                             wf2[2 * c + j % 2][:, :, bass.ds(it * 2 * P + (j // 2) * P, P)])
            yp = y_prompt[0].rearrange("(b p) d -> p b d", p=P)
            ys = y_sample.rearrange("b s d -> (b s) d")
            for n in (6, 7):
                sp.wait_ge(y_half, n + 1)
                sp.dma_start(yp[:, :, n * P:(n + 1) * P], y_tok[:, n % 2, :, :]).then_inc(y_last, 16)
                sp.wait_ge(y_copied, n + 1 + 2)
                sp.dma_start(ys[:, n * P:(n + 1) * P], ys_tok[:, n % 2, :]).then_inc(y_last, 16)
            sp.wait_ge(y_last, 16 * 4)
            sp.wait_ge(copies, 16 * 48)
            sp.wait_ge(new_rows, 16 * 7)
            sp.wait_ge(conv_out, 16 * 2)
            sp.wait_ge(kv_stored, 16 * 6 * 4)
            sp.wait_ge(new_stored, 16 * 3 * 4)
            sp.wait_ge(gates_stored, 16 * 4)
            for slot in range(2):
                sp.wait_ge(y_out[slot], 16 * 2 * 3)

        def qkv_pair(pe, unit, tt, t2):
            def cnt(per_t, n):
                return at_(per_t * t2 + n, 2 * per_t, tt)

            tb = [0]

            def bank():
                n = tb[0]
                tb[0] += 1
                pe.wait_ge(tb_free, cnt(TB_PER_T, n + 1))
                return 6 + n % 2

            def project(i):
                if i < 2:
                    pe.wait_ge(o_norm, cnt(8, 2))
                elif i == 2:
                    pe.wait_ge(gate_copied, cnt(2, 2))
                else:
                    pe.wait_ge(norm_done, cnt(6, i - 2))
                unit(U_QKV + PER_T * t2 + i, 2 * PER_T, tt, pair(i % 3), x_high, x_low).then_inc(unit_done, 1)

            gate_at = [0]

            def gate_parts(count):
                for _ in range(count):
                    f, k = gate_at[0] // KT, gate_at[0] % KT
                    gate_at[0] += 1
                    if k == 0:
                        pe.wait_ge(gate_copied, cnt(2, f + 2))
                    mm = unit(U_QKV + PER_T * t2 + 9 + f, 2 * PER_T, tt, pair(2), x_high, x_low, part=k)
                    if k == KT - 1:
                        mm.then_inc(unit_done, 1)

            def sums(i):
                pe.wait_ge(sq_done, cnt(6, i + 1))
                for h in range(2):
                    mm = pe.matmul(ps[:, bank(), 0:HT], head_ones[:, :], square[:, i % 2, h * HT:(h + 1) * HT], start=True, stop=True)
                mm.then_inc(tb_full, 2)

            def kv_transposes(src):
                nb = bank()
                for blk in range(NB):
                    mm = pe.transpose(ps[:, nb, blk * P:(blk + 1) * P], src[:, blk * P:(blk + 1) * P], ident[:, :])
                mm.then_inc(tb_full, 1)

            def new_transposes(srcs):
                nb = bank()
                for g in range(G):
                    mm = pe.transpose(ps[0:TS, nb, g * P:(g + 1) * P], srcs[:, g, TP:T], ident[:, :])
                mm.then_inc(tb_full, 1)

            def score(j):
                hh, b = j // 4, j % 4
                hp = slice(hh * E, (hh + 1) * E)
                if j:
                    pe.wait_ge(exp_done, cnt(8, j))
                for g in range(G):
                    k0 = (max(b - 1, 0) if g == 0 else 0) * P
                    n = (b + 1) * P - k0
                    mm = pe.matmul(ps[:, g, 512 - n:512], qk[hp, g, b * P:(b + 1) * P], qk[hp, 3 + g, k0:k0 + n], start=True, stop=True)
                mm.then_inc(scores, 1)

            def blocks(j):
                b = j % 4
                return [(0, kb) for kb in range(max(b - 1, 0), b + 1)] + [(g, kb) for g in (1, 2) for kb in range(b + 1)]

            tbp = [0]

            def attend(j):
                hh = j // 4
                bl = blocks(j)
                groups = [bl[i:i + 4] for i in range(0, len(bl), 4)]
                pe.wait_ge(exp_done, cnt(8, j + 1))

                def turn(gi):
                    nb = bank()
                    for n in range(len(groups[gi])):
                        c0 = (4 * gi + n) * P
                        mm = pe.transpose(ps[:, nb, n * P:(n + 1) * P], probs[:, j % 2, c0:c0 + P], ident[:, :])
                    mm.then_inc(tb_full, 1)

                base = tb[0]
                for gi in range(min(2, len(groups))):
                    turn(gi)
                gate_parts(GATE_PARTS[j][0])
                pe.wait_ge(o_norm, cnt(8, j + 2))
                for gi in range(len(groups)):
                    pe.wait_ge(tb_free, cnt(TB_PER_T, base + gi + 1 + 2))
                    if gi + 2 < len(groups):
                        turn(gi + 2)
                    for n, (g, kb) in enumerate(groups[gi]):
                        c0 = (4 * gi + n) * P
                        mm = pe.matmul(ps[:, 3, 0:E], probs_t[:, j % 2, c0:c0 + P], v_tok[:, kb, g, hh * E:(hh + 1) * E],
                                       start=(gi == 0 and n == 0), stop=(4 * gi + n == len(bl) - 1))
                    if gi == 0 and len(groups) > 1:
                        gate_parts(GATE_PARTS[j][1])
                mm.then_inc(o_done, 1)
                if len(groups) == 1:
                    gate_parts(GATE_PARTS[j][1])

            for i in range(8):
                if i == 2:
                    pe.wait_ge(u_done, 8 + 2)
                project(i)
                if 1 <= i <= 6:
                    sums(i - 1)
            for i in (3, 4):
                if i == 3:
                    pe.wait_ge(norm_done, cnt(6, 5))
                kv_transposes(qk[:, i, :])
            project(8)
            pe.wait_ge(norm_done, cnt(6, 6))
            kv_transposes(qk[:, 5, :])
            pe.wait_ge(v_done, cnt(3, 2))
            score(0)
            kv_transposes(v_feat[:, 0, :])
            kv_transposes(v_feat[:, 1, :])
            new_transposes(qk[:, 0:G, :])
            pe.wait_ge(v_done, cnt(3, 3))
            kv_transposes(v_feat[:, 2, :])
            new_transposes(qk[:, G:2 * G, :])
            new_transposes(v_feat[:, :, :])
            gate_parts(4)
            pe.wait_ge(tb_free, cnt(TB_PER_T, 19 + 2))
            for j in range(8):
                if j < 7:
                    score(j + 1)
                attend(j)
            pe.wait_ge(o_norm, cnt(8, 8 + 2))
            nb = bank()
            for b in range(NB):
                mm = pe.transpose(ps[:, nb, b * P:(b + 1) * P], o_tok[:, b, :], ident[:, :])
            mm.then_inc(tb_full, 1)
            assert tb[0] == TB_PER_T and gate_at[0] == 2 * KT


        @block.tensor
        def _(pe):
            def unit(a, b, it, out, high, low, ready=None, k0=0, first=True, last=True, cols=None, part=None):
                if not part:
                    pe.wait_ge(split_done, at_(a + 1 + 2, b, it))
                wh, wl = w_high[a % 2], w_low[a % 2]
                nk = KT
                if cols is not None:
                    nk = 4
                    wh = wh[:, :, :].rearrange("p k n -> p (k n)").rearrange("p (k n) -> p k n", k=4)
                    wl = wl[:, :, :].rearrange("p k n -> p (k n)").rearrange("p (k n) -> p k n", k=4)
                for k in (range(nk) if part is None else (part,)):
                    if ready is not None:
                        ready(k)
                    n0 = 0 if cols is None else cols
                    for n, (w, x) in enumerate(((wh, high), (wh, low), (wl, high))):
                        for h in range(2):
                            mm = pe.matmul(out[:, h, :], w[:, k, n0:n0 + P], x[:, k0 + k, h * HT:(h + 1) * HT],
                                           start=(first and k == 0 and n == 0), stop=(last and k == nk - 1 and n == 2))
                return mm

            pe.wait_ge(consts, 1)
            pe.wait_ge(chan_in, 16 * 5)
            for k in range(KT):
                mm = pe.transpose(ps[:, 3, k * NCV:(k + 1) * NCV], chan_rows[:, k * P:(k + 1) * P], ident[0:NCV, 0:NCV])
            mm.then_inc(chan_tr, 1)
            for i in range(5):
                n = P if i < NB else TS
                pe.wait_ge(x_scaled, i + 1)
                if i == 1:
                    pe.wait_ge(chan_done, 1)
                if i >= 2:
                    pe.wait_ge(x_low_done, i - 1)
                for k in range(KT):
                    mm = pe.transpose(ps[:, 2 * (i % 2) + k // 4, (k % 4) * P:(k % 4) * P + n],
                                      xn_tok[0:n, i % 2, k * P:(k + 1) * P], ident[0:n, 0:n])
                mm.then_inc(x_tr, 1)
            pe.wait_ge(state_in, 16)
            for k in range(KT):
                for h in range(2):
                    mm = pe.transpose(ps[:, 4 + k // 2, (k % 2) * 240 + h * 120:(k % 2) * 240 + (h + 1) * 120],
                                      state_rows[:, h, k * P:(k + 1) * P], ident[0:120, 0:120])
            mm.then_inc(state_tr, 1)
            pe.wait_ge(x_low_done, 5)
            pe.wait_ge(state_done, 1)

            with pe.Fori(0, 4) as it:
                for j in range(4):
                    pe.wait_ge(u_done, at_(j // 2 + 1, 2, it))
                    unit(U_GLU + j, 4, it, pair(j), x_high, x_low).then_inc(unit_done, 1)
            pe.wait_ge(u_done, 7 + 2)
            pe.wait_ge(pool_c, 7)

            with pe.Fori(0, 2) as tt:
                for t2 in range(2):
                    qkv_pair(pe, unit, tt, t2)
            pe.wait_ge(o_norm, 2 + 32)

            def tile(n, b, it):
                pe.wait_ge(tile_free, at_(n + 1, b, it))
                return pair(n % 2)

            for j in range(8):
                unit(U_CGATE + j, 0, 0, tile(j, 0, 0), x_high, x_low).then_inc(unit_done, 1)
                if j == 0:
                    pe.wait_ge(c_summed, 1 + KT)
                    for h in range(2):
                        for odd in range(2):
                            mm = pe.matmul(ps[:, 4 + h, 0:HT], ones[:, :], c_sum[:, odd, h * HT:(h + 1) * HT], start=odd == 0, stop=odd == 1)
                    mm.then_inc(mean_done, 1)
                if j == 1:
                    pe.wait_ge(tb_free, 2 + 4 * TB_PER_T)
                    for k in range(KT):
                        mm = pe.transpose(ps[0:CW - 1 + TS, 6 + k // 4, (k % 4) * P:(k % 4 + 1) * P],
                                          u_in[:, k, TP:UW], ident[:, :])
                    mm.then_inc(ut_done, 1)
                if j == 3:
                    pe.wait_ge(csq_sum, KT)
                    pe.wait_ge(ut_copied, 1)
                    for h in range(2):
                        mm = pe.matmul(ps[:, 6 + h, 0:HT], ones[:, :], ln_sum[:, h * HT:(h + 1) * HT], start=True, stop=True)
                    mm.then_inc(var_done, 1)

            for j in range(8):
                unit(U_COUT + j, 0, 0, tile(8 + j, 0, 0), c_high, c_low,
                     ready=(lambda k: pe.wait_ge(c_low_done, k + 1)) if j == 0 else None).then_inc(unit_done, 1)
                if j == 0:
                    pe.wait_ge(s_red, 2 * G)
                    pe.wait_ge(centred, KT)
                    at = 0
                    for g in range(G):
                        n = SROWS[g]
                        mm = pe.transpose(ps[0:64, 4, at:at + n], s_score[0:n, g, :], ident[0:n, 0:n])
                        at += n
                    mm.then_inc(s_tr, 1)
                if j == 1:
                    pe.wait_ge(s_pn, 1)
                    at = 0
                    for g in range(G):
                        n = SROWS[g]
                        mm = pe.transpose(ps[0:n, 5, g * 64:(g + 1) * 64], s_prob[:, at:at + n], ident[0:64, 0:64])
                        at += n
                    mm.then_inc(s_ptr, 1)
            pe.wait_ge(v_sum, 5)
            pe.wait_ge(ln_rs, 1)
            for ct in range(4):
                for b in range(TS):
                    mm = pe.matmul(ps[:, 6, ct * TS + b:ct * TS + b + 1], qbuf[:, b, ct * P:(ct + 1) * P], ones[:, 0:1],
                                   start=True, stop=True)
            mm.then_inc(s_pv, 1)
            pe.wait_ge(tile_free, 16 + 2)
            pe.wait_ge(s_out, 1)
            with pe.Fori(0, 2) as it:
                for j in range(2):
                    for c in range(2):
                        n = 2 * j + c
                        pe.wait_ge(tile_free, at_(16 + n - 1, 4, it))
                        mm = unit(U_AOUT + j, 2, it, pair(n), o_high, o_low, cols=c * P,
                                  ready=(lambda k: pe.wait_ge(o_low_done, 2)) if j == 0 and c == 0 else None)
                    mm.then_inc(unit_done, 1)
            pe.wait_ge(x2_in, 32)
            pe.wait_ge(tile_free, 24 + 2)
            for k in range(KT):
                if k >= 3:
                    pe.wait_ge(xt_copied, k - 2)
                for b in range(NB):
                    mm = pe.transpose(ps[:, 4 + k % 3, b * P:(b + 1) * P], x_tok2[:, b, k * P:(k + 1) * P], ident[:, :])
                mm.then_inc(xt_full, 1)
            for k in range(KT):
                mm = pe.transpose(ps[:, 7, k * TS:(k + 1) * TS], x_tok2[0:TS, NB, k * P:(k + 1) * P], ident[0:TS, 0:TS])
            mm.then_inc(xt_full, 1)
            with pe.Fori(0, 2) as it:
                for j in range(4):
                    unit(U_WO + j, 4, it, tile(24 + j, 4, it), c_high, c_low,
                         ready=(lambda k: pe.wait_ge(m_low, k + 1)) if j == 0 else None).then_inc(unit_done, 1)

            for c in range(2):
                base = U_FF + 32 * c
                tiles = 32 + 24 * c
                if c == 0:
                    for j in range(4):
                        unit(base + j, 0, 0, tile(tiles + j, 0, 0), x_high, x_low,
                             ready=(lambda k: pe.wait_ge(hn_low, k + 1)) if j == 0 else None).then_inc(unit_done, 1)
                        if j == 0:
                            pe.wait_ge(hss_sum, KT + 2)
                            pe.wait_ge(xt_copied, KT + 1)
                            for h in range(2):
                                mm = pe.matmul(ps[:, 4 + h, 0:HT], ones[:, :], h_ss[:, h * HT:(h + 1) * HT], start=True, stop=True)
                            mm.then_inc(hss_done, 1)
                with pe.Fori(1 - c, 4) as it:
                    for j in range(4):
                        unit(base + j, 4, it, tile(tiles + j, 4, it), x_high, x_low).then_inc(unit_done, 1)
                def ff2(it, peeled=False):
                    for j in range(4):
                        n = j // 2
                        if j % 2 == 0:
                            out = tile(tiles + 16 + n, 2, it)
                        mm = unit(base + 16 + j, 4, it, out, hid_high, hid_low, k0=8 * (j % 2), first=(j % 2 == 0), last=(j % 2 == 1),
                                  ready=(lambda k: pe.wait_ge(hid_lo, 16 * c + 8 * (j % 2) + k + 1)) if n == 0 else None)
                        mm.then_inc(unit_done, 1)

                def y_transposes(n, b, it):
                    pe.wait_ge(tile_free, at_(tiles + 16 + n + 1 + 2, b, it))
                    pe.wait_ge(y_copied, at_(n + 1, b, it))
                    for blk in range(NB):
                        pe.transpose(ps[:, 4 + n % 2, blk * P:(blk + 1) * P], y_feat[:, n % 2, blk * P:(blk + 1) * P], ident[:, :])
                    pe.transpose(ps[0:TS, 6 + n % 2, 0:P], y_feat[:, n % 2, TP:T], ident[:, :]).then_inc(y_tr, 1)

                if c == 0:
                    with pe.Fori(0, 4) as it:
                        ff2(it)
                else:
                    def ff2_last(b, it, with_prev):
                        for j in range(4):
                            n = j // 2
                            if j % 2 == 0:
                                out = tile(tiles + 16 + n, b, it)
                            mm = unit(base + 16 + j, 2 * b, it, out, hid_high, hid_low, k0=8 * (j % 2), first=(j % 2 == 0), last=(j % 2 == 1),
                                      ready=(lambda k: pe.wait_ge(hid_lo, 16 * c + 8 * (j % 2) + k + 1)) if n == 0 else None)
                            mm.then_inc(unit_done, 1)
                            if j == 2:
                                y_transposes(0, b, it)
                            if j == 0 and with_prev:
                                y_transposes(-1, b, it)
                    ff2_last(0, 0, False)
                    with pe.Fori(1, 4) as it:
                        ff2_last(2, it, True)
                    y_transposes(7, 0, 0)

        def ln_silu(act, k):
            act.wait_ge(ln_scaled, k + 1)
            act.activation(conv[:, k, :], conv[:, k, :], ACT.Silu, scale=chan[:, k, C_LNG:C_LNG + 1],
                           bias=chan[:, k, C_LNB:C_LNB + 1]).then_inc(silu_done, 1)
            act.wait_ge(silu_done, k + 1)
            act.activation(c_high[:, k, :], conv[:, k, :], ACT.Copy).then_inc(c_high_done, 1)

        def act_pair(act, cast, done, tt, t2):
            def cnt(per_t, n):
                return at_(per_t * t2 + n, 2 * per_t, tt)

            def next_cast(i):
                cast(U_QKV + PER_T * t2 + i + 2, 2 * PER_T, tt)

            tb = [0]

            def copy_bank(dst, np_, ncols, view=None):
                n = tb[0]
                tb[0] += 1
                act.wait_ge(tb_full, cnt(TB_PER_T, n + 1))
                src = ps[0:np_, 6 + n % 2, 0:ncols]
                if view:
                    src = src.rearrange("p (b c) -> p b c", c=P)
                return act.activation(dst, src, ACT.Copy)

            def root(i):
                tb[0] += 2
                act.wait_ge(tb_full, cnt(TB_PER_T, tb[0]))
                act.activation(halves(rstd[:, i % 2, :]), ps[:, 6:8, 0:HT], ACT.Ln, scale=1.0 / E, bias=eps_col[:, :]).then_inc(tb_free, 2)
                act.wait_ge(tb_free, cnt(TB_PER_T, tb[0] + 2))
                act.activation(rstd[:, i % 2, :], rstd[:, i % 2, :], ACT.Exp, scale=-0.5).then_inc(rs_done, 1)

            for i in range(9):
                if i == 8:
                    act.wait_ge(rows_free, cnt(1, 1))
                    copy_bank(k_tok[:, :, 0, :], P, 512, True).then_inc(tb_free, 1)
                    copy_bank(k_tok[:, :, 1, :], P, 512, True).then_inc(tb_free, 1)
                next_cast(i)
                done(U_QKV + PER_T * t2 + i, 2 * PER_T, tt)
                if i < 6:
                    act.activation(halves(square[:, i % 2, :]), pair(i % 3), ACT.Square).then_inc(sq_done, 1)
                else:
                    act.activation(halves(v_feat[:, i - 6, :]), pair(i % 3), ACT.Copy).then_inc(v_done, 1)
                if 1 <= i <= 6:
                    if i >= 3:
                        act.wait_ge(norm_done, cnt(6, i - 2))
                    root(i - 1)
            copy_bank(k_tok[:, :, 2, :], P, 512, True).then_inc(tb_free, 1)
            copy_bank(v_tok[:, :, 0, :], P, 512, True).then_inc(tb_free, 1)
            copy_bank(v_tok[:, :, 1, :], P, 512, True).then_inc(tb_free, 1)
            copy_bank(new_tok[:, 0, :, :], TS, G * P, True).then_inc(tb_free, 1)
            copy_bank(v_tok[:, :, 2, :], P, 512, True).then_inc(tb_free, 1)
            copy_bank(new_tok[:, 1, :, :], TS, G * P, True).then_inc(tb_free, 1)
            copy_bank(new_tok[:, 2, :, :], TS, G * P, True).then_inc(tb_free, 1)

            def exponent(j):
                b = j % 4
                act.wait_ge(max_done, cnt(8, j + 1))
                at = 0
                for g in range(G):
                    n = (min(b, 1) + 1 if g == 0 else b + 1) * P
                    a = act.activation(probs[:, j % 2, at:at + n], ps[:, g, 512 - n:512], ACT.Exp,
                                       bias=job_max[:, j % 2, 3:4], accum_out=job_sum[:, j % 2, g:g + 1])
                    at += n
                a.then_inc(exp_done, 1)

            exponent(0)
            for j in range(8):
                b = j % 4
                n = (min(b, 1) + 1) + 2 * (b + 1)
                for c0 in range(0, n, 4):
                    m = min(4, n - c0)
                    copy_bank(probs_t[:, j % 2, c0 * P:(c0 + m) * P], P, m * P).then_inc(tb_free, 1)
                if j + 1 < 8:
                    exponent(j + 1)
                if j in GATE_JOB:
                    f = GATE_JOB.index(j)
                    next_cast(9 + f)
                    act.activation(halves(gate_stage[:, f, :]), pair(2), ACT.Copy).then_inc(gate_copied, 1)
            copy_bank(attn[:, bass.ds(tt * 2 + t2, 1), 0:TP].rearrange("p o c -> p (o c)"), P, 512).then_inc(tb_free, 1)
            assert tb[0] == TB_PER_T, tb

        @block.scalar
        def _(act):
            def cast(a, b, it):
                act.wait_ge(raw_full[a % 2], at_(16 * (a // 2 + 1), 8 * b, it))
                act.wait_ge(unit_done, at_(a + 1, b, it))
                act.activation(w_high[a % 2][:, :, :], w_raw[a % 2][:, :, :], ACT.Copy).then_inc(cast_done, 1)

            def done(a, b, it):
                act.wait_ge(unit_done, at_(a + 1 + 2, b, it))

            act.wait_ge(consts, 1)
            act.wait_ge(dve_c, 1)
            for i in range(5):
                n = P if i < NB else TS
                act.wait_ge(x_in[i], 16)
                if i:
                    act.wait_ge(x_sq, i)
                act.activation(junk[0:n, :], x_tok[0:n, i, :], ACT.Square, accum_out=x_ss[0:n, i:i + 1]).then_inc(x_sq, 1)
                if i:
                    act.wait_ge(x_var, i)
                    act.activation(x_rstd[:, i - 1:i], x_rstd[:, i - 1:i], ACT.Sqrt).then_inc(x_sd, 1)
            act.wait_ge(x_var, 5)
            act.activation(x_rstd[:, 4:5], x_rstd[:, 4:5], ACT.Sqrt).then_inc(x_sd, 1)
            cast(0, 0, 0)
            cast(1, 0, 0)
            act.wait_ge(chan_tr, 1)
            act.activation(chan[:, :, :], ps[:, 3, 0:KT * NCV], ACT.Copy).then_inc(chan_done, 1)
            for i in range(5):
                n = P if i < NB else TS
                act.wait_ge(x_tr, i + 1)
                act.activation(x_high[:, :, i * P:i * P + n],
                               ps[:, 2 * (i % 2):2 * (i % 2) + 2, :].rearrange("p h (k c) -> p (h k) c", k=4)[:, :, 0:n],
                               ACT.Copy).then_inc(x_high_done, 1)
            act.wait_ge(state_tr, 1)
            act.activation(state[:, :, :, :].rearrange("p (h k) b r -> p h (k b r)", h=4), ps[:, 4:8, 0:480], ACT.Copy).then_inc(state_done, 1)

            with act.Fori(0, 4) as it:
                for j in range(4):
                    cast(U_GLU + j + 2, 4, it)
                    if j % 2:
                        done(U_GLU + j, 4, it)
                        act.wait_ge(u_done, at_(j // 2 + 1, 2, it))
                        act.activation(halves(glu_sig[:, j // 2, :]), pair(j), ACT.Sigmoid).then_inc(glu_sig_done, 1)

            with act.Fori(0, 2) as tt:
                for t2 in range(2):
                    act_pair(act, cast, done, tt, t2)

            def ln_square(k):
                act.wait_ge(centred, k + 1)
                if k >= 4:
                    act.wait_ge(csq_sum, k - 3)
                act.activation(ln_sq[:, k % 4, :], conv[:, k, :], ACT.Square).then_inc(csq_done, 1)

            for j in range(8):
                cast(U_CGATE + j + 2, 0, 0)
                if j == 2:
                    act.wait_ge(ut_done, 1)
                    act.activation(state_out[:, :].rearrange("r (h c) -> r h c", h=2), ps[0:CW - 1 + TS, 6:8, :], ACT.Copy).then_inc(ut_copied, 1)
                if j == 3:
                    act.wait_ge(var_done, 1)
                    act.activation(halves(ln_rstd[:, :]), ps[:, 6:8, 0:HT], ACT.Ln, bias=eps_col[:, :]).then_inc(ln_sd, 1)
                    act.wait_ge(ln_sd, 1)
                    act.activation(ln_rstd[:, :], ln_rstd[:, :], ACT.Exp, scale=-0.5).then_inc(ln_rs, 1)
                if j in (4, 5):
                    for k in range(4 * (j - 4), 4 * (j - 3)):
                        ln_silu(act, k)
                done(U_CGATE + j, 0, 0)
                act.activation(halves(gate_c[:, j, :]), pair(j % 2), ACT.Sigmoid).then_inc(tile_free, 1)
                if j in (0, 1):
                    for k in range(4 * j, 4 * (j + 1)):
                        ln_square(k)
            for j in range(8):
                cast(U_COUT + j + 2, 0, 0)
                if j == 2:
                    act.wait_ge(c_low_done, KT)
                    act.activation(o_high[:, :, 0:TP], attn[:, :, 0:TP], ACT.Copy).then_inc(o_high_done, 1)
                if j == 0:
                    act.wait_ge(s_mx, 2)
                    act.activation(s_prob[:, :], ps[0:64, 4, 0:SKEYS], ACT.Exp, bias=s_small[0:64, 5:6],
                                   accum_out=s_small[0:64, 6:7]).then_inc(s_exp, 1)
                if j == 1:
                    act.wait_ge(s_ptr, 1)
                    act.activation(s_prob_t[:, 0:2, :], ps[:, 5, 0:128].rearrange("p (g c) -> p g c", g=2), ACT.Copy).then_inc(s_ptc, 1)
                    act.activation(s_prob_t[0:SROWS[2], 2, :], ps[0:SROWS[2], 5, 128:192], ACT.Copy).then_inc(s_ptc, 1)
            act.wait_ge(s_pv, 1)
            act.activation(attn[:, :, TP:T], ps[:, 6, 0:4 * TS].rearrange("p (t b) -> p t b", t=4), ACT.Copy,
                           scale=float(D)).then_inc(s_out, 1)
            act.wait_ge(s_out, 1)
            act.activation(o_high[:, :, TP:T], attn[:, :, TP:T], ACT.Copy).then_inc(o_high_done, 1)
            act.wait_ge(gates_in, 16)
            for k in range(0, KT, 2):
                act.activation(gate_a[:, k:k + 2, :], gate_a[:, k:k + 2, :], ACT.Sigmoid).then_inc(agate_done, 2)
            with act.Fori(0, 2) as it:
                for j in range(2):
                    cast(U_AOUT + j + 2, 2, it)
                    for c in range(2):
                        n = 2 * j + c
                        act.wait_ge(merged, at_(n + 1, 4, it))
                        act.activation(c_high[:, bass.ds(it * 4 + n, 1), :], gate_a[:, bass.ds(it * 4 + n, 1), :], ACT.Copy).then_inc(m_high, 1)
            for k in range(KT):
                act.wait_ge(xt_full, k + 1)
                act.activation(x_feat[:, k, 0:TP], ps[:, 4 + k % 3, :], ACT.Copy).then_inc(xt_copied, 1)
            act.wait_ge(xt_full, KT + 1)
            act.activation(x_feat[:, :, TP:T], ps[:, 7, 0:KT * TS].rearrange("p (k c) -> p k c", k=KT), ACT.Copy).then_inc(xt_copied, 1)
            with act.Fori(0, 2) as it:
                for j in range(4):
                    cast(U_WO + j + 2, 4, it)
                    act.wait_ge(tile_free, at_(24 + j + 1 + 2, 4, it))
                    act.wait_ge(hss_sum, at_(j + 1, 4, it))
                    act.activation(h_sq[:, j % 2, :], h_feat[:, bass.ds(it * 4 + j, 1), :].rearrange("p o c -> p (o c)"), ACT.Square).then_inc(hsq_done, 1)
                    act.activation(x_high[:, bass.ds(it * 4 + j, 1), :], h_feat[:, bass.ds(it * 4 + j, 1), :], ACT.Copy,
                                   scale=chan[:, bass.ds(it * 4 + j, 1), C_N2:C_N2 + 1].rearrange("p o c -> p (o c)")).then_inc(hn_high, 1)
            for c in range(2):
                base = U_FF + 32 * c
                act.wait_ge(tile_free, 32 + 24 * c + 2)
                with act.Fori(0, 4) as it:
                    for j in range(4):
                        cast(base + j + 2, 4, it)
                        done(base + j, 4, it)
                        act.wait_ge(hid_done, at_(16 * c + j + 1, 4, it))
                        act.activation(halves(relu[:, j % 2, :]), pair(j % 2), ACT.Relu).then_inc(tile_free, 1)
                        act.wait_ge(tile_free, at_(32 + 24 * c + j + 1 + 2, 4, it))
                        act.activation(relu[:, j % 2, :], relu[:, j % 2, :], ACT.Square).then_inc(rsq_done, 1)
                        act.wait_ge(hid_done, at_(16 * c + j + 1 + 2, 4, it))
                        act.activation(hid_high[:, bass.ds(it * 4 + j, 1), :], hid[:, j % 2, :].rearrange("p (o c) -> p o c", o=1), ACT.Copy).then_inc(hid_hi, 1)
                if c == 0:
                    with act.Fori(0, 4) as it:
                        for j in range(4):
                            cast(base + 16 + j + 2, 4, it)
                else:
                    def y_copy(n):
                        act.wait_ge(y_tr, n + 1)
                        if n >= 2:
                            act.wait_ge(y_out[n % 2], 32 * (n // 2))
                        act.activation(y_tok[:, n % 2, :, :].rearrange("p b c -> p (b c)"), ps[:, 4 + n % 2, :], ACT.Copy).then_inc(y_half, 1)
                        act.activation(ys_tok[:, n % 2, :], ps[0:TS, 6 + n % 2, 0:P], ACT.Copy).then_inc(y_copied, 1)

                    for u in range(16):
                        if u < 14:
                            cast(base + 16 + u + 2, 0, 0)
                        if u % 2 and u >= 3:
                            y_copy(u // 2 - 1)
                    y_copy(7)

        def x_part(dve, i):
            n = P if i < NB else TS
            dve.wait_ge(x_high_done, i + 1)
            dve.tensor_tensor(x_low[:, :, i * P:i * P + n],
                              ps[:, 2 * (i % 2):2 * (i % 2) + 2, :].rearrange("p h (k c) -> p (h k) c", k=4)[:, :, 0:n],
                              x_high[:, :, i * P:i * P + n].bitcast(F32), ALU.subtract).then_inc(x_low_done, 1)

        def tap(dve, n, k, before):
            dst = conv[:, bass.ds(n, 1), 0:TP].rearrange("p o c -> p (o c)")
            src = u_in[:, bass.ds(n, 1), k:k + TP].rearrange("p o c -> p (o c)")
            w = chan[:, bass.ds(n, 1), k:k + 1].rearrange("p o c -> p (o c)")
            if k == 0:
                dve.tensor_scalar(dst, src, w, chan[:, bass.ds(n, 1), C_BIAS:C_BIAS + 1].rearrange("p o c -> p (o c)"),
                                  ALU.mult, ALU.add).then_inc(tap_done, 1)
            else:
                dve.wait_ge(tap_done, before)
                dve.scalar_tensor_tensor(dst, src, w, dst, ALU.mult, ALU.add).then_inc(tap_done, 1)

        def c_part(dve, k):
            dve.wait_ge(c_high_done, k + 1)
            dve.tensor_tensor(c_low[:, k, :], conv[:, k, :], c_high[:, k, :].bitcast(F32), ALU.subtract).then_inc(c_low_done, 1)

        def sample_scores(dve, g, h):
            n = SROWS[g]
            dve.wait_ge(kq_done, 2 * g + h + 1)
            kb = (kbuf2, kbuf, kbuf2)[g]
            dve.tensor_reduce(s_score[0:n, g, 32 * h:32 * (h + 1)], kb[0:n, 4 * h:4 * (h + 1), :].rearrange("p b (h e) -> p (b h) e", e=E),
                              AX.X, ALU.add).then_inc(s_red, 1)

        def by_head(buf, n, b0, b1):
            return buf[0:n, b0:b1, :].rearrange("p b (h e) -> p (b h) e", e=E)

        def prob_of(g, n, b0, b1):
            return bass.AP(s_prob_t, g * TS * HEADS + b0 * HEADS, [[G * TS * HEADS, n], [1, (b1 - b0) * HEADS], [0, E]])

        def dve_pair(dve, split, tt, t2):
            def cnt(per_t, n):
                return at_(per_t * t2 + n, 2 * per_t, tt)

            cuts = conv_schedule()
            per_t = sum(len(c) for c in cuts)
            made = [0]

            def taps(slot):
                for tile, k in cuts[slot]:
                    n = tt * 4 + 2 * t2 + tile
                    before = at_(8 * GLU_TAPS + per_t * t2 + made[0] - 1, 2 * per_t, tt)
                    tap(dve, n, k, before)
                    made[0] += 1

            def norm(i):
                dve.wait_ge(rs_done, cnt(6, i + 1))
                dve.scalar_tensor_tensor(halves(qk[:, i, :]), pair(i % 3), qk_gain[:, i:i + 1], halves(rstd[:, i % 2, :]),
                                         ALU.mult, ALU.mult).then_inc(norm_done, 1)

            for i in range(9):
                split(U_QKV + PER_T * t2 + i + 2, 2 * PER_T, tt)
                if 1 <= i <= 6:
                    norm(i - 1)
                if i < 8:
                    taps(i)

            def maximum(j):
                b = j % 4
                dve.wait_ge(scores, cnt(8, j + 1))
                dve.memset(job_sum[:, j % 2, 0:3], 0.0)
                for g in range(G):
                    n = (min(b, 1) + 1 if g == 0 else b + 1) * P
                    dve.tensor_tensor_reduce(ps[:, g, 512 - n:512], ps[:, g, 512 - n:512], mask[:, g, 512 - n:512], 1.0,
                                             LOWEST, ALU.add, ALU.max, job_max[:, j % 2, g:g + 1]).then_inc(masked, 1)
                dve.wait_ge(masked, cnt(24, 3 * j + 3))
                dve.tensor_reduce(job_max[:, j % 2, 3:4], job_max[:, j % 2, 0:3], AX.X, ALU.max, negate=True).then_inc(max_done, 1)

            def finish(j):
                dve.wait_ge(exp_done, cnt(8, j + 1))
                dve.tensor_reduce(job_sum[:, j % 2, 3:4], job_sum[:, j % 2, 0:3], AX.X, ALU.add).then_inc(sum_done, 1)
                dve.wait_ge(sum_done, cnt(8, j + 1))
                dve.reciprocal(job_sum[:, j % 2, 3:4], job_sum[:, j % 2, 3:4]).then_inc(rsum_done, 1)
                dve.wait_ge(rsum_done, cnt(8, j + 1))
                dve.wait_ge(o_done, cnt(8, j + 1))
                dve.tensor_scalar(o_tok[:, j % 4, (j // 4) * E:(j // 4 + 1) * E], ps[:, 3, 0:E], job_sum[:, j % 2, 3:4],
                                  None, ALU.mult).then_inc(o_norm, 1)

            maximum(0)
            taps(8)
            for j in range(8):
                if j + 1 < 8:
                    maximum(j + 1)
                taps(9 + j)
                finish(j)
                if j in GATE_JOB:
                    split(U_QKV + PER_T * t2 + 9 + GATE_JOB.index(j) + 2, 2 * PER_T, tt)


        @block.vector
        def _(dve):
            def split(a, b, it):
                dve.wait_ge(cast_done, at_(a + 1, b, it))
                dve.tensor_tensor(w_low[a % 2][:, :, :], w_raw[a % 2][:, :, :], w_high[a % 2][:, :, :].bitcast(F32),
                                  ALU.subtract).then_inc(split_done, 1)

            def done(a, b, it):
                dve.wait_ge(unit_done, at_(a + 1 + 2, b, it))

            for i, (s, n) in enumerate(((split_done, 2), (unit_done, 2), (tile_free, 2), (tb_free, 2),
                                        (o_norm, 2), (u_done, 2), (y_copied, 2), (rows_free, 1))):
                dve.memset(credit[:, i:i + 1], 0.0).then_inc(s, n)
            dve.memset(s_small[:, 3:4], 0.0).then_inc(gate_copied, 2)
            dve.memset(s_small[:, 0:1], 0.0).then_inc(hid_done, 2)
            dve.memset(s_small[:, 1:2], 0.0).then_inc(hss_sum, 2)
            dve.memset(x_ss[:, :], 1.0).then_inc(dve_c, 1)

            dve.wait_ge(dve_c, 1)

            def x_variance(i):
                dve.wait_ge(x_sq, i + 1)
                dve.tensor_scalar(x_rstd[:, i:i + 1], x_ss[:, i:i + 1], 1.0 / D, EPS, ALU.mult, ALU.add).then_inc(x_var, 1)

            def x_scale(i):
                n = P if i < NB else TS
                if i >= 2:
                    dve.wait_ge(x_tr, i - 1)
                dve.scalar_tensor_tensor(xn_tok[0:n, i % 2, :], x_tok[0:n, i, :], x_rinv[0:n, i:i + 1], gain1[0:n, :],
                                         ALU.mult, ALU.mult).then_inc(x_scaled, 1)

            x_variance(0)
            for i in range(5):
                if i + 1 < 5:
                    x_variance(i + 1)
                dve.wait_ge(x_sd, i + 1)
                dve.reciprocal(x_rinv[:, i:i + 1], x_rstd[:, i:i + 1]).then_inc(x_rs, 1)
                if i == 0:
                    dve.wait_ge(gain_in, 16)
                if i < 2:
                    dve.wait_ge(x_rs, i + 1)
                    x_scale(i)
            dve.wait_ge(x_rs, 5)
            for i in range(2, 5):
                x_scale(i)
                if i == 2:
                    split(0, 0, 0)
                    split(1, 0, 0)
                x_part(dve, i - 2)
            x_part(dve, 3)
            x_part(dve, 4)

            dve.wait_ge(qkg_in, 16 * 12)
            dve.tensor_scalar(qk_gain[:, 0:G], qk_gain[:, 0:G], E ** -0.5, None, ALU.mult).then_inc(mask_done, 1)

            dve.wait_ge(chan_done, 1)
            dve.wait_ge(pool_c, 11)
            n = 1
            for g in (1, 2):
                dve.tensor_scalar(dist_mod[:, :], dist[:, :], DIL[g] - 1, None, ALU.bitwise_and).then_inc(mask_done, 1)
                dve.wait_ge(mask_done, n + 1)
                dve.tensor_scalar(mod_mask[:, :], dist_mod[:, :], 0.0, NEG, ALU.is_gt, ALU.mult).then_inc(mask_done, 1)
                dve.wait_ge(mask_done, n + 2)
                dve.tensor_copy(mask[:, g, 0:3 * P].rearrange("p (b c) -> p b c", b=3), bass.AP(mod_mask, 0, [[P, P], [0, 3], [1, P]])).then_inc(mask_done, 1)
                dve.tensor_tensor(mask[:, g, 3 * P:4 * P], mod_mask[:, :], mask[:, 0, 3 * P:4 * P], ALU.min).then_inc(mask_done, 1)
                n += 4
                dve.wait_ge(mask_done, n)

            dve.wait_ge(state_done, 1)
            sc = conv[:, :, TP:T]
            taps_b = bass.AP(chan, 0, [[KT * NCV, P], [NCV, KT], [0, TS], [1, CW - 1]])
            last_b = bass.AP(chan, CW - 1, [[KT * NCV, P], [NCV, KT], [0, TS]])
            bias_b = bass.AP(chan, C_BIAS, [[KT * NCV, P], [NCV, KT], [0, TS]])
            dve.tensor_tensor(state[:, :, :, :], state[:, :, :, :], taps_b, ALU.mult).then_inc(sconv, 1)
            dve.wait_ge(sconv, 1)
            dve.tensor_reduce(sc, state[:, :, :, :], AX.X, ALU.add).then_inc(sconv, 1)

            def glu_taps(n, second, part, it):
                for k in range(part * GLU_TAPS // 2, (part + 1) * GLU_TAPS // 2):
                    tap(dve, n, k, at_(second * GLU_TAPS + k, 2 * GLU_TAPS, it))

            with dve.Fori(0, 4) as it:
                for j in range(4):
                    split(U_GLU + j + 2, 4, it)
                    n = it * 2 + j // 2
                    if j % 2:
                        dve.wait_ge(glu_sig_done, at_(j // 2 + 1, 2, it))
                        dve.tensor_tensor(halves(u_in[:, bass.ds(n, 1), CW - 1:UW].rearrange("p o c -> p (o c)")), pair(j - 1),
                                          halves(glu_sig[:, j // 2, :]), ALU.mult).then_inc(u_done, 1)
                        dve.wait_ge(u_done, at_(j // 2 + 1 + 2, 2, it))
                        glu_taps(n, j // 2, 0, it)
                        if j == 3:
                            glu_taps(n, 1, 1, it)
                    elif j == 2:
                        glu_taps(it * 2, 0, 1, it)

            dve.tensor_tensor(glu_sig[:, 0, 0:64].rearrange("p (k b) -> p k b", k=KT), u_in[:, :, CW - 1 + TP:UW], last_b, ALU.mult).then_inc(sconv, 1)
            dve.wait_ge(sconv, 3)
            dve.tensor_tensor(sc, sc, glu_sig[:, 0, 0:64].rearrange("p (k b) -> p k b", k=KT), ALU.add).then_inc(sconv, 1)
            dve.wait_ge(sconv, 4)
            dve.tensor_tensor(sc, sc, bias_b, ALU.add).then_inc(sconv, 1)

            with dve.Fori(0, 2) as tt:
                for t2 in range(2):
                    dve_pair(dve, split, tt, t2)

            for j in range(8):
                split(U_CGATE + j + 2, 0, 0)
                if j in (0, 1):
                    dve.wait_ge(mean_done, 1)
                    for k in range(4 * j, 4 * (j + 1)):
                        dve.tensor_tensor(halves(conv[:, k, :]), halves(conv[:, k, :]), ps[:, 4:6, 0:HT], ALU.subtract).then_inc(centred, 1)
                if j in (1, 2):
                    for k in range(4 * (j - 1), 4 * j):
                        dve.wait_ge(csq_done, k + 1)
                        if k == 0:
                            dve.tensor_copy(ln_sum[:, :], ln_sq[:, 0, :]).then_inc(csq_sum, 1)
                        else:
                            dve.wait_ge(csq_sum, k)
                            dve.tensor_tensor(ln_sum[:, :], ln_sum[:, :], ln_sq[:, k % 4, :], ALU.add).then_inc(csq_sum, 1)
                if j == 3:
                    dve.wait_ge(ln_rs, 1)
                if j in (3, 4):
                    for k in range(4 * (j - 3), 4 * (j - 2)):
                        dve.tensor_tensor(conv[:, k, :], conv[:, k, :], ln_rstd[:, :], ALU.mult).then_inc(ln_scaled, 1)
                if j == 5:
                    for k in range(KT):
                        c_part(dve, k)
                for g, h in ((), (), ((0, 0),), ((0, 1),), ((1, 0),), (), ((1, 1), (2, 0)), ((2, 1),))[j]:
                    sample_scores(dve, g, h)
            for j in range(8):
                if j == 0:
                    dve.wait_ge(tile_free, 8 + 2)
                split(U_COUT + j + 2, 0, 0)
                done(U_COUT + j, 0, 0)
                gc = halves(gate_c[:, j, :])
                dve.tensor_tensor(gc, pair(j % 2), gc, ALU.mult).then_inc(tile_free, 1)
                if j == 2:
                    dve.wait_ge(s_ptc, 2)
                    dve.wait_ge(v_in[1], 16)
                    for h in range(2):
                        qh = by_head(qbuf, P, 4 * h, 4 * h + 4)
                        dve.tensor_tensor(qh, qh, prob_of(1, P, 4 * h, 4 * h + 4), ALU.mult).then_inc(v_sum, 1)
                if j in (4, 5):
                    h = j - 4
                    dve.wait_ge(v_weighted, 1)
                    dve.wait_ge(v_sum, 2)
                    qh = by_head(qbuf, P, 4 * h, 4 * h + 4)
                    dve.tensor_tensor(qh, qh, by_head(kbuf, P, 4 * h, 4 * h + 4), ALU.add).then_inc(v_sum, 1)
                if j == 6:
                    dve.wait_ge(v_weighted, 2)
                    dve.wait_ge(v_sum, 4)
                    qh = by_head(qbuf, SROWS[2], 0, TS)
                    dve.tensor_tensor(qh, qh, by_head(kbuf2, SROWS[2], 0, TS), ALU.add).then_inc(v_sum, 1)
                if j == 3:
                    dve.wait_ge(o_high_done, 1)
                    dve.tensor_tensor(o_low[:, :, 0:TP], attn[:, :, 0:TP], o_high[:, :, 0:TP].bitcast(F32), ALU.subtract).then_inc(o_low_done, 1)
                if j == 0:
                    dve.wait_ge(s_tr, 1)
                    dve.reduce_max(s_small[0:64, 4:5], ps[0:64, 4, 0:SKEYS], AX.X).then_inc(s_mx, 1)
                    dve.wait_ge(s_mx, 1)
                    dve.tensor_scalar(s_small[0:64, 5:6], s_small[0:64, 4:5], -1.0, None, ALU.mult).then_inc(s_mx, 1)
                    dve.wait_ge(s_exp, 1)
                    dve.reciprocal(s_small[0:64, 7:8], s_small[0:64, 6:7]).then_inc(s_rs, 1)
                    dve.wait_ge(s_rs, 1)
                    dve.tensor_scalar(s_prob[:, :], s_prob[:, :], s_small[0:64, 7:8], None, ALU.mult).then_inc(s_pn, 1)
            dve.wait_ge(o_high_done, 2)
            dve.tensor_tensor(o_low[:, :, TP:T], attn[:, :, TP:T], o_high[:, :, TP:T].bitcast(F32), ALU.subtract).then_inc(o_low_done, 1)
            dve.wait_ge(agate_done, KT)
            with dve.Fori(0, 2) as it:
                for j in range(2):
                    split(U_AOUT + j + 2, 2, it)
                    done(U_AOUT + j, 2, it)
                    for c in range(2):
                        n = 2 * j + c
                        ga3 = gate_a[:, bass.ds(it * 4 + n, 1), :]
                        ga = halves(ga3.rearrange("p o c -> p (o c)"))
                        dve.tensor_tensor(ga, pair(n), ga, ALU.mult).then_inc(tile_free, 1)
                    for c in range(2):
                        n = 2 * j + c
                        dve.wait_ge(m_high, at_(n + 1, 4, it))
                        dve.tensor_tensor(c_low[:, bass.ds(it * 4 + n, 1), :], gate_a[:, bass.ds(it * 4 + n, 1), :],
                                          c_high[:, bass.ds(it * 4 + n, 1), :].bitcast(F32), ALU.subtract).then_inc(m_low, 1)
            with dve.Fori(0, 2) as it:
                for j in range(4):
                    split(U_WO + j + 2, 4, it)
                    done(U_WO + j, 4, it)
                    dve.wait_ge(xt_copied, KT + 1)
                    n = bass.ds(it * 4 + j, 1)
                    dve.tensor_tensor(halves(h_feat[:, n, :].rearrange("p o c -> p (o c)")), pair(j % 2),
                                      halves(x_feat[:, n, :].rearrange("p o c -> p (o c)")), ALU.add).then_inc(tile_free, 1)
                    dve.wait_ge(tile_free, at_(24 + j + 1 + 2, 4, it))
                    dve.wait_ge(hn_high, at_(j + 1, 4, it))
                    dve.scalar_tensor_tensor(x_low[:, n, :].rearrange("p o c -> p (o c)"), h_feat[:, n, :].rearrange("p o c -> p (o c)"),
                                             chan[:, n, C_N2:C_N2 + 1].rearrange("p o c -> p (o c)"),
                                             x_high[:, n, :].bitcast(F32).rearrange("p o c -> p (o c)"), ALU.mult, ALU.subtract).then_inc(hn_low, 1)
            for c in range(2):
                base = U_FF + 32 * c

                def ff1(b, it):
                    for j in range(4):
                        split(base + j + 2, b, it)
                        if c == 0 and b == 0 and j == 0:
                            dve.wait_ge(hss_done, 1)
                            dve.tensor_scalar(halves(h_rs2[:, :]), ps[:, 4:6, 0:HT], EPS, None, ALU.add).then_inc(h_rs, 1)
                            dve.wait_ge(h_rs, 1)
                            dve.reciprocal(h_rs2[:, :], h_rs2[:, :]).then_inc(h_rs, 1)
                            dve.wait_ge(h_rs, 2)
                        dve.wait_ge(rsq_done, at_(16 * c + j + 1, b, it))
                        dve.tensor_tensor(hid[:, j % 2, :], relu[:, j % 2, :], h_rs2[:, :], ALU.mult).then_inc(hid_done, 1)
                        dve.wait_ge(hid_hi, at_(16 * c + j + 1, b, it))
                        n = bass.ds(it * b + j, 1)
                        dve.tensor_tensor(hid_low[:, n, :].rearrange("p o c -> p (o c)"), hid[:, j % 2, :],
                                          hid_high[:, n, :].bitcast(F32).rearrange("p o c -> p (o c)"), ALU.subtract).then_inc(hid_lo, 1)

                if c == 0:
                    ff1(0, 0)
                with dve.Fori(1 - c, 4) as it:
                    ff1(4, it)
                dve.wait_ge(tile_free, 48 + 24 * c + 2)
                if c == 0:
                    with dve.Fori(0, 4) as it:
                        for j in range(4):
                            split(base + 16 + j + 2, 4, it)
                            if j % 2:
                                done(base + 16 + j, 4, it)
                                hf = halves(h_feat[:, bass.ds(it * 2 + j // 2, 1), :].rearrange("p o c -> p (o c)"))
                                dve.tensor_tensor(hf, pair(j // 2), hf, ALU.add).then_inc(tile_free, 1)
                else:
                    for n in range(8):
                        for j in (2 * n, 2 * n + 1):
                            if j < 14:
                                split(base + 16 + j + 2, 0, 0)
                        done(base + 16 + 2 * n + 1, 0, 0)
                        if n >= 2:
                            dve.wait_ge(y_tr, n - 1)
                        dve.tensor_tensor(halves(y_feat[:, n % 2, :]), pair(n % 2), halves(h_feat[:, n, :]), ALU.add).then_inc(tile_free, 1)

        @block.gpsimd
        def _(pool):
            made = [0]

            def link(ins):
                made[0] += 1
                ins.then_inc(pool_c, 1)
                pool.wait_ge(pool_c, made[0])

            link(pool.memset(ident[:, :], 0.0))
            pool.affine_select(out=ident[:, :], in_=ident[:, :], compare_op=ALU.not_equal, fill=1.0, base=0,
                               pattern=[[-1, P]], channel_multiplier=1).then_inc(pool_c, 1)
            made[0] += 1
            pool.memset(eps_col[:, :], EPS).then_inc(pool_c, 1)
            made[0] += 1
            pool.wait_ge(pool_c, made[0])
            pool.memset(ones[:, :], 1.0 / D).then_inc(consts, 1)
            link(pool.memset(head_ones[:, :], 0.0))
            link(pool.memset(head_ones[0:E, 0:E], 1.0))
            link(pool.memset(head_ones[E:P, E:P], 1.0))
            link(pool.memset(mask[:, 0, :], 0.0))
            pool.memset(u_in[:, :, 0:CW - 1], 0.0).then_inc(pool_c, 1)
            pool.affine_select(out=mask[:, 0, 2 * P:3 * P], in_=mask[:, 0, 2 * P:3 * P], compare_op=ALU.is_ge, fill=NEG, base=0,
                               pattern=[[1, P]], channel_multiplier=-1).then_inc(pool_c, 1)
            made[0] += 2
            pool.affine_select(out=mask[:, 0, 3 * P:4 * P], in_=mask[:, 0, 3 * P:4 * P], compare_op=ALU.is_ge, fill=NEG, base=0,
                               pattern=[[-1, P]], channel_multiplier=1).then_inc(pool_c, 1)
            pool.iota(dist[:, :], pattern=[[-1, P]], base=P, channel_multiplier=1).then_inc(pool_c, 1)
            for half in range(2):
                hp = slice(half * E, (half + 1) * E)
                for g in range(G):
                    pool.dma_start(qk_gain[hp, g:g + 1], q_norm_g[0, g].rearrange("(e o) -> e o", o=1)).then_inc(qkg_in, 16)
                    pool.dma_start(qk_gain[hp, G + g:G + g + 1], k_norm_g[0, g].rearrange("(e o) -> e o", o=1)).then_inc(qkg_in, 16)

            def cache_tile(src, g):
                a = rows(src[g])
                if g == 0:
                    return a.rearrange("b r c -> r b c")
                d = DIL[g]
                return a.rearrange("b (r d) c -> r d b c", d=d)[:, 0, :, :]

            pool.wait_ge(sconv, 5)
            pool.memset(c_sum[:, :, :], 0.0).then_inc(c_summed, 1)
            pool.dma_start(kbuf2[:, :, :], cache_tile(cache_k, 0)).then_inc(k_in, 16)

            with pool.Fori(0, 4) as t:
                col = bass.ds(t * P, P)
                pool.wait_ge(tb_free, t * TB_PER_T + 21 + 2)
                for src, dst in ((k_tok, pk), (v_tok, pv)):
                    pool.dma_start(rows(dst[0])[0][:, col], src[:, NB - 1, 0, :]).then_inc(kv_stored, 16)
                    for g in (1, 2):
                        pool.dma_start(rows(dst[g])[0].rearrange("(b p) c -> p b c", p=P)[:, :, col], src[:, :, g, :]).then_inc(kv_stored, 16)
                for n in range(3):
                    pool.dma_start(scratch[n][:, :, col], new_tok[:, n, :, :]).then_inc(new_stored, 16)
                pool.wait_ge(gate_copied, 2 * t + 4)
                pool.dma_start(gate_rows[:, bass.ds(t * 2, 2), :], gate_stage[:, :, :]).then_inc(gates_stored, 16)
                pool.wait_ge(tap_done, 8 * GLU_TAPS + 2 * (CW - GLU_TAPS) * (t + 1))
                pool.wait_ge(c_summed, 2 * t + 1)
                pool.tensor_tensor(pool_mark[:, 1:2], eps_col[:, :], eps_col[:, :], ALU.mult).then_inc(pool_c, 1)
                for odd in range(2):
                    pool.tensor_tensor(c_sum[:, odd, :], c_sum[:, odd, :], conv[:, bass.ds(t * 2 + odd, 1), :].rearrange("p o c -> p (o c)"),
                                       ALU.add).then_inc(c_summed, 1)
                pool.wait_ge(gates_stored, 16 * t + 16)
                pool.wait_ge(kv_stored, 96 * t + 96)
                pool.wait_ge(new_stored, 48 * t + 48)
                pool.tensor_tensor(pool_mark[:, 0:1], eps_col[:, :], eps_col[:, :], ALU.mult).then_inc(rows_free, 1)

            qrow, krow, vrow = scratch[0], scratch[1], scratch[2]

            def load_queries(g, h):
                n = (128, 128, 64)[g]
                b0 = 4 * h
                if g:
                    pool.wait_ge(kq_done, 2 * (g - 1) + h + 1)
                pool.dma_start(qbuf[0:n, b0:b0 + 4, :],
                               bass.AP(qrow.tensor, qrow.offset + g * AW + b0 * G * AW, [[0, n], [G * AW, 4], [1, AW]])).then_inc(q_in[h], 16)
                if g == 2:
                    pool.dma_start(qbuf[64:67, b0:b0 + 4, :], qrow[b0:b0 + 4].rearrange("b g c -> g b c")).then_inc(q_in[h], 16)

            def product(g, h):
                n = SROWS[g]
                kb = (kbuf2, kbuf, kbuf2)[g][0:n, 4 * h:4 * h + 4, :]
                pool.wait_ge(q_in[h], 16 * (g + 1 + g // 2))
                if h == 0:
                    pool.wait_ge(k_in, 16 * (g + 1 + g // 2))
                pool.tensor_tensor(kb, kb, qbuf[0:n, 4 * h:4 * h + 4, :], ALU.mult).then_inc(kq_done, 1)

            pool.wait_ge(tb_free, 2 + 4 * TB_PER_T)
            load_queries(0, 0)
            load_queries(0, 1)
            pool.dma_start(kbuf[:, :, :], cache_tile(cache_k, 1)).then_inc(k_in, 16)
            product(0, 0)
            load_queries(1, 0)
            product(0, 1)
            load_queries(1, 1)
            product(1, 0)
            load_queries(2, 0)
            product(1, 1)
            load_queries(2, 1)
            pool.wait_ge(s_red, 2)
            pool.dma_start(kbuf2[0:64, :, :], cache_tile(cache_k, 2)).then_inc(k_in, 16)
            pool.dma_start(kbuf2[64:67, :, :], krow.rearrange("b g c -> g b c")).then_inc(k_in, 16)
            product(2, 0)
            product(2, 1)
            pool.wait_ge(kq_done, 6)
            pool.dma_start(qbuf[:, :, :], cache_tile(cache_v, 1)).then_inc(v_in[1], 16)
            pool.wait_ge(s_red, 4)
            pool.dma_start(kbuf[:, :, :], cache_tile(cache_v, 0)).then_inc(v_in[0], 16)
            pool.wait_ge(ut_copied, 1)
            pool.dma_start(p_conv[0, 0], state_out[0:CW - 1, :]).then_inc(conv_out, 16)
            pool.dma_start(s_conv[0][:, CW - 2, :], state_out[CW - 1:CW - 1 + TS, :]).then_inc(conv_out, 16)
            pool.wait_ge(s_red, 6)
            pool.dma_start(kbuf2[0:64, :, :], cache_tile(cache_v, 2)).then_inc(v_in[2], 16)
            pool.dma_start(kbuf2[64:67, :, :], vrow.rearrange("b g c -> g b c")).then_inc(vn_in, 16)
            pool.dma_start(s_conv[0][:, 0:CW - 2, :], state_conv[0][:, 1:CW - 1, :]).then_inc(new_rows, 16)
            for g in range(G):
                at_row = CACHE[g] - 1 if g < 2 else CACHE[g]
                pool.dma_start(rows(sk[g])[:, at_row, :], krow[:, g, :]).then_inc(new_rows, 16)
                pool.dma_start(rows(sv[g])[:, at_row, :], vrow[:, g, :]).then_inc(new_rows, 16)
            pool.wait_ge(s_ptc, 2)
            pool.wait_ge(v_in[0], 16)
            vb = by_head(kbuf, P, 0, TS)
            pool.tensor_tensor(vb, vb, prob_of(0, P, 0, TS), ALU.mult).then_inc(v_weighted, 1)
            pool.wait_ge(v_in[2], 16)
            pool.wait_ge(vn_in, 16)
            vb = by_head(kbuf2, SROWS[2], 0, TS)
            pool.tensor_tensor(vb, vb, prob_of(2, SROWS[2], 0, TS), ALU.mult).then_inc(v_weighted, 1)
            pool.wait_ge(v_sum, 5)
            pool.dma_start(gate_a[:, :, :], gate_rows).then_inc(gates_in, 16)
            pool.wait_ge(s_pv, 1)
            pool.dma_start(x_tok2[:, 0:NB, :], x_prompt[0].rearrange("(b p) d -> p b d", p=P)).then_inc(x2_in, 16)
            pool.dma_start(x_tok2[0:TS, NB, :], x_sample.rearrange("b s d -> (b s) d")).then_inc(x2_in, 16)
            for n in range(KT):
                pool.wait_ge(tile_free, 16 + n + 1 + 2)
                pool.tensor_tensor(gate_a[:, n, :], gate_a[:, n, :], gate_c[:, n, :], ALU.add).then_inc(merged, 1)
            for k in range(KT):
                pool.wait_ge(hsq_done, k + 1)
                if k == 0:
                    pool.tensor_copy(h_ss[:, :], h_sq[:, 0, :]).then_inc(hss_sum, 1)
                else:
                    pool.wait_ge(hss_sum, k + 2)
                    pool.tensor_tensor(h_ss[:, :], h_ss[:, :], h_sq[:, k % 2, :], ALU.add).then_inc(hss_sum, 1)
            yp = y_prompt[0].rearrange("(b p) d -> p b d", p=P)
            ys = y_sample.rearrange("b s d -> (b s) d")
            for n in range(6):
                pool.wait_ge(y_half, n + 1)
                pool.wait_ge(y_copied, n + 1 + 2)
                pool.dma_start(yp[:, :, n * P:(n + 1) * P], y_tok[:, n % 2, :, :]).then_inc(y_out[n % 2], 16)
                pool.dma_start(ys[:, n * P:(n + 1) * P], ys_tok[:, n % 2, :]).then_inc(y_out[n % 2], 16)


def at_(a, b=0, it=0):
    return a + b * it if b else a


_INS = ['x_prompt', 'x_sample', 'cache_k1', 'cache_v1', 'cache_k2', 'cache_v2', 'cache_k3', 'cache_v3', 'state_conv',
        'norm1_g', 'w_in', 'q_norm_g', 'k_norm_g', 'conv_w', 'conv_b', 'conv_ln_g', 'conv_ln_b', 'w_attn_out',
        'w_conv_out', 'w_o', 'norm2_g', 'w_ff1', 'w_ff2']
_OUTS = [(1, TP, D), (TS, 1, D),
         (1, 1, 128, HEADS, E), (1, 1, 128, HEADS, E), (1, 1, TP, HEADS, E), (1, 1, TP, HEADS, E),
         (1, 1, TP, HEADS, E), (1, 1, TP, HEADS, E), (1, 1, CW - 1, D),
         (1, TS, 128, HEADS, E), (1, TS, 128, HEADS, E), (1, TS, 512, HEADS, E), (1, TS, 512, HEADS, E),
         (1, TS, 1025, HEADS, E), (1, TS, 1025, HEADS, E), (1, TS, CW - 1, D)]


def kernel(**inputs):
    import numpy as _np
    import concourse.bacc as _bacc
    from concourse import mybir as _mybir
    from concourse.bass_utils import run_bass_kernel_spmd as _run

    nc = _bacc.Bacc("TRN2", target_bir_lowering=False, num_devices=1)
    arrays, args = {}, []
    for name in _INS:
        a = _np.ascontiguousarray(inputs[name])
        arrays[f"in_{name}_dram"] = a
        args.append(nc.dram_tensor(f"in_{name}_dram", a.shape, _mybir.dt.from_np(a.dtype), kind="ExternalInput").ap())
    for i, shape in enumerate(_OUTS):
        args.append(nc.dram_tensor(f"out_{i}_dram", shape, _mybir.dt.float32, kind="ExternalOutput").ap())
    build_step(nc, *args)
    r = _run(nc, [arrays], core_ids=[0])
    return tuple(r.results[0][f"out_{i}_dram"] for i in range(len(_OUTS)))
```
